# Optimizing a Trainium2 kernel written in Bass

```python
import math
import jax
import jax.numpy as jnp
from jax import lax
import numpy as np

D_MODEL = 2048
BATCH = 1
SEQ = 512
DEPTH = 1
DEC_BATCH = 8
DEC_SEQ = 4
PAST_LEN = 2048
PAGE_SIZE = 128

HEAD_DIM = 128
MIX_WIDTH = D_MODEL
ATT_WIDTH = MIX_WIDTH // 2
N_ATT_HEADS = ATT_WIDTH // HEAD_DIM
SGU_WIDTH = MIX_WIDTH - ATT_WIDTH
N_SGU_GROUPS = SGU_WIDTH // HEAD_DIM
CHUNK = 128
BRANCHES = ((128, 1), (512, 4), (2048, 16))
ATT_WINDOW = max(w for w, _ in BRANCHES)
BAND = 128
N_KEYS = 128
N_EXPERTS = N_KEYS * N_KEYS
PEER_HEADS = 8
PEER_TOPK = 16
D_QUERY = 256
D_QHALF = D_QUERY // 2
TOK_BLOCK = 128
EPS = 1e-6
IN_SPLITS = (ATT_WIDTH, 2 * ATT_WIDTH, 3 * ATT_WIDTH, 3 * ATT_WIDTH + SGU_WIDTH)
IN_WIDTH = 3 * ATT_WIDTH + 2 * SGU_WIDTH

kernel_name = 'hybrid_dilated_sgu_peer_step'

def rmsnorm(x, g):
    xf = x.astype(jnp.float32)
    y = xf * lax.rsqrt(jnp.mean(xf * xf, axis=-1, keepdims=True) + EPS)
    return (y * g.astype(jnp.float32)).astype(x.dtype)

def layernorm(x, g, b):
    xf = x.astype(jnp.float32)
    mu = jnp.mean(xf, axis=-1, keepdims=True)
    var = jnp.mean(jnp.square(xf - mu), axis=-1, keepdims=True)
    y = (xf - mu) * lax.rsqrt(var + EPS)
    return (y * g.astype(jnp.float32) + b.astype(jnp.float32)).astype(x.dtype)

def alibi_slopes(n):
    return 2.0 ** (-8.0 * jnp.arange(1, n + 1, dtype=jnp.float32) / n)

def adaln(c, w_ada, b_ada):
    m = (jax.nn.silu(c) @ w_ada + b_ada)[:, None, :]
    return jnp.split(m, 6, axis=-1)

def dilated_branch_prompt(q, k, v, dil, n_steps, slopes):
    B, S, H, Dh = q.shape
    span = BAND * dil
    Sp = -(-S // span) * span
    L = Sp // dil
    nb = L // BAND

    def to_blocks(t):
        t = jnp.pad(t, ((0, 0), (0, Sp - S), (0, 0), (0, 0)))
        t = t.reshape(B, L, dil, H, Dh).transpose(0, 2, 1, 3, 4)
        return t.reshape(B, dil, nb, BAND, H, Dh)

    def with_prev(t):
        prev = jnp.pad(t, ((0, 0), (0, 0), (1, 0), (0, 0), (0, 0), (0, 0)))[:, :, :-1]
        return jnp.concatenate([prev, t], axis=3)

    qb = to_blocks(q)
    kw = with_prev(to_blocks(k))
    vw = with_prev(to_blocks(v))
    s = jnp.einsum('brnqhc,brnkhc->brnhqk', qb, kw).astype(jnp.float32) * (HEAD_DIM ** -0.5)
    a = jnp.arange(BAND)[:, None]
    kk = jnp.arange(2 * BAND)[None, :]
    steps = BAND + a - kk
    valid = (steps >= 0) & (steps <= n_steps)
    not_before_start = (jnp.arange(nb)[:, None, None] > 0) | (kk >= BAND)[None]
    mask = valid[None] & not_before_start
    bias = -slopes[:, None, None] * (dil * steps).astype(jnp.float32)[None]
    s = jnp.where(mask[:, None], s + bias, -jnp.inf)
    lse = jax.nn.logsumexp(s, axis=-1)
    p = jnp.exp(s - lse[..., None])
    o = jnp.einsum('brnhqk,brnkhc->brnqhc', p.astype(vw.dtype), vw).astype(jnp.float32)
    o = o.reshape(B, dil, L, H, Dh).transpose(0, 2, 1, 3, 4).reshape(B, Sp, H, Dh)[:, :S]
    lse = lse.transpose(0, 1, 2, 4, 3).reshape(B, dil, L, H).transpose(0, 2, 1, 3).reshape(B, Sp, H)[:, :S]
    return o, lse

def dilated_branch_sample(q, k_all, v_all, dil, n_steps, slopes, buf_len):
    T = q.shape[1]
    steps = jnp.arange(n_steps + 1)
    idx = buf_len + jnp.arange(T)[:, None] - dil * steps[None, :]
    valid = idx >= 0
    idx = jnp.maximum(idx, 0)
    kg = jnp.take(k_all, idx, axis=1)
    vg = jnp.take(v_all, idx, axis=1)
    s = jnp.einsum('bthc,btkhc->bthk', q, kg).astype(jnp.float32) * (HEAD_DIM ** -0.5)
    bias = -slopes[:, None] * (dil * steps).astype(jnp.float32)[None, :]
    s = jnp.where(valid[None, :, None, :], s + bias[None, None], -jnp.inf)
    lse = jax.nn.logsumexp(s, axis=-1)
    p = jnp.exp(s - lse[..., None])
    o = jnp.einsum('bthk,btkhc->bthc', p.astype(vg.dtype), vg).astype(jnp.float32)
    return o, lse

def combine_branches(res, dtype):
    o = jnp.stack([r[0] for r in res])
    lse = jnp.stack([r[1] for r in res])
    w = jax.nn.softmax(lse, axis=0)
    o = jnp.sum(w[..., None] * o, axis=0)
    return o.reshape(o.shape[0], o.shape[1], ATT_WIDTH).astype(dtype)

def sgu_mix_prompt(vn, ws, bs):
    B, S, _ = vn.shape
    vr = vn.reshape(B, S // CHUNK, CHUNK, N_SGU_GROUPS, HEAD_DIM)
    m = jnp.einsum('gts,bnsgc->bntgc', ws, vr) + bs.T[:, :, None]
    return m.reshape(B, S, SGU_WIDTH)

def sgu_mix_sample(vn, ws, bs):
    B, T, _ = vn.shape
    vr = vn.reshape(B, T, N_SGU_GROUPS, HEAD_DIM)
    m = jnp.einsum('gts,bsgc->btgc', ws[:, :T, :T], vr) + bs[:, :T].T[:, :, None]
    return m.reshape(B, T, SGU_WIDTH)

def peer_ffn(h, w_query, sub_keys, expert_u, expert_v):
    T = h.shape[0]
    Tp = -(-T // TOK_BLOCK) * TOK_BLOCK
    hb_all = jnp.pad(h, ((0, Tp - T), (0, 0))).reshape(Tp // TOK_BLOCK, TOK_BLOCK, D_MODEL)
    kk = PEER_TOPK * PEER_TOPK

    def block(hb):
        q = (hb @ w_query).reshape(TOK_BLOCK, PEER_HEADS, 2, D_QHALF)
        sc = jnp.einsum('thpc,pnc->thpn', q, sub_keys).astype(jnp.float32)
        top_s, top_i = lax.top_k(sc, PEER_TOPK)
        cand_s = (top_s[:, :, 0, :, None] + top_s[:, :, 1, None, :]).reshape(TOK_BLOCK, PEER_HEADS, kk)
        cand_i = (top_i[:, :, 0, :, None] * N_KEYS + top_i[:, :, 1, None, :]).reshape(TOK_BLOCK, PEER_HEADS, kk)
        best_s, best_j = lax.top_k(cand_s, PEER_TOPK)
        idx = jnp.take_along_axis(cand_i, best_j, axis=-1)
        gate = jax.nn.softmax(best_s, axis=-1)
        u = expert_u[idx]
        act = jax.nn.gelu(jnp.einsum('thkd,td->thk', u, hb).astype(jnp.float32), approximate=False)
        coef = (gate * act).astype(hb.dtype)
        return jnp.einsum('thk,thkd->td', coef, expert_v[idx])

    return lax.map(block, hb_all).reshape(Tp, D_MODEL)[:T]

def layer_forward(x, c, mixer, w_ada, b_ada, g_norm1, w_in, ln_v_g, ln_v_b, w_out, g_norm2,
                  w_query, sub_keys, expert_u, expert_v):
    B, S, _ = x.shape
    sh1, sc1, gt1, sh2, sc2, gt2 = adaln(c, w_ada, b_ada)
    h = rmsnorm(x, g_norm1) * (1.0 + sc1) + sh1
    q, k, v, u, g = jnp.split(h @ w_in, IN_SPLITS, axis=-1)
    heads = lambda t: t.reshape(B, S, N_ATT_HEADS, HEAD_DIM)
    u = jax.nn.gelu(u, approximate=False)
    vn = layernorm(jax.nn.gelu(g, approximate=False), ln_v_g, ln_v_b)
    att, gate_v, states = mixer(heads(q), heads(k), heads(v), vn)
    mix = jnp.concatenate([att, u * gate_v], axis=-1)
    x = x + gt1 * (mix @ w_out)
    h2 = rmsnorm(x, g_norm2) * (1.0 + sc2) + sh2
    ffn = peer_ffn(h2.reshape(B * S, D_MODEL), w_query, sub_keys, expert_u, expert_v).reshape(B, S, D_MODEL)
    x = x + gt2 * ffn
    return x, states

def setup_inputs(seed: int = 0) -> dict:
    key = jax.random.key(seed)
    ks = jax.random.split(key, 24)
    f32 = jnp.float32

    def nrm(k, shape, s=1.0):
        return s * jax.random.normal(k, shape, dtype=f32)

    buf = min(ATT_WINDOW, PAST_LEN)
    return {
        'x_prompt': nrm(ks[0], (BATCH, SEQ, D_MODEL)),
        'x_sample': nrm(ks[1], (DEC_BATCH, DEC_SEQ, D_MODEL)),
        'cache_k': nrm(ks[2], (DEPTH, DEC_BATCH, buf, N_ATT_HEADS, HEAD_DIM)),
        'cache_v': nrm(ks[3], (DEPTH, DEC_BATCH, buf, N_ATT_HEADS, HEAD_DIM)),
        'c_prompt': nrm(ks[4], (BATCH, D_MODEL)),
        'c_sample': nrm(ks[5], (DEC_BATCH, D_MODEL)),
        'w_ada': nrm(ks[6], (DEPTH, D_MODEL, 6 * D_MODEL), 0.5 * D_MODEL ** -0.5),
        'b_ada': nrm(ks[7], (DEPTH, 6 * D_MODEL), 0.01),
        'g_norm1': 1.0 + nrm(ks[8], (DEPTH, D_MODEL), 0.02),
        'w_in': nrm(ks[9], (DEPTH, D_MODEL, IN_WIDTH), D_MODEL ** -0.5),
        'ln_v_g': 1.0 + nrm(ks[10], (DEPTH, SGU_WIDTH), 0.02),
        'ln_v_b': nrm(ks[11], (DEPTH, SGU_WIDTH), 0.01),
        'w_spatial': nrm(ks[12], (DEPTH, N_SGU_GROUPS, CHUNK, CHUNK), CHUNK ** -0.5),
        'b_spatial': 1.0 + nrm(ks[13], (DEPTH, N_SGU_GROUPS, CHUNK), 0.02),
        'w_out': nrm(ks[14], (DEPTH, MIX_WIDTH, D_MODEL), MIX_WIDTH ** -0.5),
        'g_norm2': 1.0 + nrm(ks[15], (DEPTH, D_MODEL), 0.02),
        'w_query': nrm(ks[16], (DEPTH, D_MODEL, PEER_HEADS * D_QUERY), D_MODEL ** -0.5),
        'sub_keys': nrm(ks[17], (DEPTH, 2, N_KEYS, D_QHALF), D_QHALF ** -0.5),
        'expert_u': nrm(ks[18], (DEPTH, N_EXPERTS, D_MODEL), D_MODEL ** -0.5),
        'expert_v': nrm(ks[19], (DEPTH, N_EXPERTS, D_MODEL), 0.5),
        'g_final': 1.0 + nrm(ks[20], (D_MODEL,), 0.02),
    }

def reference(x_prompt, x_sample, cache_k, cache_v, c_prompt, c_sample, w_ada, b_ada, g_norm1, w_in,
              ln_v_g, ln_v_b, w_spatial, b_spatial, w_out, g_norm2, w_query, sub_keys, expert_u, expert_v,
              g_final):
    slopes = alibi_slopes(N_ATT_HEADS)
    tri = jnp.tril(jnp.ones((CHUNK, CHUNK), dtype=bool))
    buf_len = cache_k.shape[2]
    win_p = min(ATT_WINDOW, x_prompt.shape[1])
    xp, xs = x_prompt, x_sample
    kp_all, vp_all, ks_all, vs_all, gs_all = [], [], [], [], []
    for l in range(DEPTH):
        ws = jnp.where(tri, w_spatial[l], 0.0).astype(w_spatial.dtype)
        bs = b_spatial[l]
        ck, cv = cache_k[l], cache_v[l]

        def prompt_mixer(q, k, v, vn):
            res = [dilated_branch_prompt(q, k, v, d, w // d, slopes) for w, d in BRANCHES]
            att = combine_branches(res, q.dtype)
            return att, sgu_mix_prompt(vn, ws, bs), (k[:, -win_p:], v[:, -win_p:])

        def sample_mixer(q, k, v, vn):
            k_all = jnp.concatenate([ck.astype(k.dtype), k], axis=1)
            v_all = jnp.concatenate([cv.astype(v.dtype), v], axis=1)
            res = [dilated_branch_sample(q, k_all, v_all, d, w // d, slopes, buf_len) for w, d in BRANCHES]
            att = combine_branches(res, q.dtype)
            return att, sgu_mix_sample(vn, ws, bs), (k, v, vn)

        params = (w_ada[l], b_ada[l], g_norm1[l], w_in[l], ln_v_g[l], ln_v_b[l], w_out[l], g_norm2[l],
                  w_query[l], sub_keys[l], expert_u[l], expert_v[l])
        xp, (kp, vp) = layer_forward(xp, c_prompt, prompt_mixer, *params)
        xs, (ksn, vsn, gsn) = layer_forward(xs, c_sample, sample_mixer, *params)
        kp_all.append(kp)
        vp_all.append(vp)
        ks_all.append(ksn)
        vs_all.append(vsn)
        gs_all.append(gsn)
    y_prompt = rmsnorm(xp, g_final)
    y_sample = rmsnorm(xs, g_final)
    return (y_prompt, y_sample, jnp.stack(kp_all), jnp.stack(vp_all), jnp.stack(ks_all), jnp.stack(vs_all), jnp.stack(gs_all))


_drawn_inputs = setup_inputs


def setup_inputs(seed=0):
    import zlib

    import numpy as np

    out = dict(_drawn_inputs(seed))
    spreads = {}
    factors = {'b_ada': 3.785,
     'ln_v_g': 2.941,
     'ln_v_b': 5.659,
     'b_spatial': 8.0,
     'g_norm2': 4.566,
     'g_final': 2.86}
    for name, (base, spread) in spreads.items():
        noise = np.random.default_rng([zlib.crc32(name.encode()), seed]).standard_normal(out[name].shape)
        drawn = base * np.exp(spread * noise) if base else spread * noise
        out[name] = jnp.asarray(drawn.astype(out[name].dtype))
    for name, factor in factors.items():
        out[name] = (out[name] * factor).astype(out[name].dtype)
    return out
```

```python
import math
from contextlib import ExitStack

import concourse.bass as bass
from concourse import mybir

F32 = mybir.dt.float32
I32 = mybir.dt.int32
U32 = mybir.dt.uint32
ALU = mybir.AluOpType
ACT = mybir.ActivationFunctionType
AX_X = mybir.AxisListType.X

P = 128
D = 2048
KD = D // P
SEQ, NB_P = 512, 4
DECB, DECT = 8, 4
NS = DECB * DECT
NTOK = SEQ + NS
BLOCKS = 5
ROWS = [P] * NB_P + [NS]
H, DH = 8, 128
AW = H * DH
G = 8
PAST = 2048
EPS = 1e-6
SCALE = DH ** -0.5
WINDOWS = ((128, 1), (512, 4), (2048, 16))
NEG = -1.0e30
NKEY = 128
PH = 8
TOPK = 16
SLOTS = PH * TOPK
NC = 512
ADA_T = 6 * D // NC
IN_T = (3 * AW + 2 * AW) // NC
OUT_T = D // NC
CH = 7
FAR = 3
NK = CH * P
NKS = NK + NS
GRP = 8
RING = 4

W0 = 0
HT0 = W0 + 2 * KD * NC
MT0 = HT0 + KD * NTOK
Q0 = MT0 + KD * NTOK
K0 = Q0 + BLOCKS * AW
V0 = K0 + BLOCKS * AW
C0 = V0 + BLOCKS * AW
WORDS = C0 + 3000


def tickets():
    order = [("c",), ("ws", 0), ("ws", 1), ("wd",), ("sk",)]
    order += [("h", b, g) for b in range(BLOCKS) for g in range(4)]
    for b in range(BLOCKS):
        order += [("m", b, 0), ("m", b, 1)]
    for b in range(BLOCKS):
        order += [("mt", b, 0), ("mt", b, 1)]
    order += [("q", 0), ("k", 0)]
    for h in range(H):
        if h + 1 < H:
            order += [("q", h + 1), ("k", h + 1)]
        order += [("p", h, j) for j in range(NB_P)]
    order += [("qs",), ("ks",)]
    for b in range(DECB):
        order += [("kt", b, h, i) for h in range(H) for i in range(2)]
        order += [("pt", b)]
    order += [("h2", b, g) for b in range(BLOCKS) for g in range(4)]
    return {key: n for n, key in enumerate(order)}


def trunk_step(nc, x_prompt, x_sample, cache_k, cache_v, c_prompt, c_sample, w_ada, b_ada, g_norm1, w_in,
               ln_v_g, ln_v_b, w_spatial, b_spatial, w_out, g_norm2, w_query, sub_keys, expert_u, expert_v,
               g_final, y_prompt, y_sample, k_win, v_win, k_new, v_new, sgu_v):
    T = tickets()
    ctx = ExitStack()
    with ctx:
        arena = ctx.enter_context(nc.sbuf_tensor("arena", [P, WORDS], F32))
        ps = ctx.enter_context(nc.psum_tensor("ps", [P, 8, NC], F32))
        mod_dram = nc.dram_tensor("modulation", (1 + DECB, 6 * D), F32, kind="Internal").ap()

        def sem(name):
            return ctx.enter_context(nc.semaphore(name))

        def at(offset, *shape, rows=P):
            n = math.prod(shape)
            v = arena[0:rows, offset:offset + n]
            if len(shape) == 2:
                v = v.rearrange("p (a b) -> p a b", b=shape[1])
            if len(shape) == 3:
                v = v.rearrange("p (a b c) -> p a b c", b=shape[1], c=shape[2])
            return v

        cursor = [C0]

        def const(*shape, rows=P):
            v = at(cursor[0], *shape, rows=rows)
            cursor[0] += math.prod(shape)
            assert cursor[0] <= WORDS
            return v

        xp, xs = x_prompt.rearrange("a s d -> (a s) d"), x_sample.rearrange("b t d -> (b t) d")
        yp, ys = y_prompt.rearrange("a s d -> (a s) d"), y_sample.rearrange("b t d -> (b t) d")
        kwp, vwp = (w.rearrange("l b s h c -> (l b s) (h c)") for w in (k_win, v_win))
        knp, vnp = (w.rearrange("l b s h c -> (l b s) (h c)") for w in (k_new, v_new))
        sgp = sgu_v.rearrange("l b t d -> (l b t) d")
        x_of = [xp[b * P:(b + 1) * P, :] for b in range(NB_P)] + [xs]
        y_of = [yp[b * P:(b + 1) * P, :] for b in range(NB_P)] + [ys]
        u_rows = expert_u.rearrange("l e d -> (l e) d")
        v_rows = expert_v.rearrange("l e d -> (l e) d")

        ident = const(P)
        c_t = const(KD, 1 + DECB)
        delta = const(SEQ)
        count_ln = const(SEQ)
        bias_s = const(NKS, rows=NS)
        bias_new = const(DECB, NS, rows=NS)
        slope_s = const(1, rows=NS)
        stat = const(64)
        bs_p = const(G)
        bs_s = const(G, rows=NS)
        sub_t = const(2, NKEY)
        iota16 = const(TOPK)
        iota_i = const(TOPK).bitcast(I32)
        idx_stage = const(2, GRP).bitcast(I32)
        act_sum = const(2, GRP)
        act_gelu = const(2, GRP)
        coef = const(2, GRP)

        mod = at(HT0, 6 * D, rows=1 + DECB)
        c_in = at(K0, D, rows=1 + DECB)
        g1_rows, g2_rows = (at(HT0 + 6 * D + D * i, D, rows=1 + DECB) for i in range(2))
        assert HT0 + 8 * D <= Q0
        w_slot = [at(W0 + s * KD * NC, KD, NC) for s in range(2)]
        tmp_i = [at(V0 + 1024 * i, NKS) for i in range(4)]

        scale1_p, shift1_p, scale1_s, shift1_s = (at(MT0 + D * i, D) for i in range(4))
        x_buf = [at(K0 + D * i, D) for i in range(2)]
        h_buf = [at(V0 + D * i, D) for i in range(2)]
        h_t = at(HT0, KD, NTOK)

        mix_t = at(MT0, KD, NTOK)
        q_all, k_all, v_all = (at(o, BLOCKS, AW) for o in (Q0, K0, V0))
        u_all, g_all = k_all, v_all
        ln_g, ln_b = at(Q0, AW), at(Q0 + AW, AW)
        ws_in, ws_t = at(Q0 + 2 * AW, G, P), at(Q0 + 3 * AW, G, P)
        wd_in, wd_t = at(Q0 + 4 * AW, G, NS, rows=NS), at(Q0 + 4 * AW + G * NS, G, NS, rows=NS)

        o = HT0
        head_bias = at(o, SEQ); o += SEQ
        q_t = [at(o + SEQ * i, SEQ) for i in range(2)]; o += 2 * SEQ
        k_t = [at(o + SEQ * i, SEQ) for i in range(2)]; o += 2 * SEQ
        prob = []
        for qi in range(NB_P):
            prob.append(at(o, (qi + 1) * P)); o += (qi + 1) * P
        prob_t = at(o, NB_P, SEQ); o += NB_P * SEQ
        assert o <= MT0

        KVW = CH * AW
        kv_k = [at(0, CH, AW), at(2 * KVW, CH, AW)]
        kv_v = [at(KVW, CH, AW), at(Q0, CH, AW)]
        key_t = [at(Q0 + KVW + NK * i, NK) for i in range(2)]
        assert Q0 + KVW + 2 * NK <= K0 + NB_P * AW and 3 * KVW + 2 * NKS + 1536 <= MT0
        o = 3 * KVW
        prob_s = [at(o + NKS * i, NKS, rows=NS) for i in range(2)]; o += 2 * NKS
        prob_st = [at(o + 256 * i, CH + 1, NS) for i in range(2)]; o += 512
        q_mask = [at(o + 256 * i, H, NS) for i in range(2)]; o += 512
        q_st = at(o, H, NS); o += 256
        k_st = at(o, H, NS)

        x1 = at(Q0, BLOCKS, D)
        gate1_p, gate1_s = at(HT0, D), at(HT0 + D, D)
        scale2_p, shift2_p = at(HT0 + 2 * D, D), at(HT0 + 3 * D, D)
        scale2_s, shift2_s = at(V0, D), at(V0 + D, D)
        part = [at(V0 + 2 * D + 512 * i, NC) for i in range(2)]
        h2 = [at(W0 + KD * NC + D * b, D) for b in range(NB_P)] + [at(HT0, D)]
        h2_t = at(MT0, KD, NTOK)

        wq_slot = [at(W0 + s * KD * 256, KD, 256) for s in range(2)]
        o = HT0 + D
        qry_t = [at(o + NTOK * i, NTOK) for i in range(2)]; o += 2 * NTOK
        top_s = at(o, BLOCKS, 2, TOPK); o += BLOCKS * 2 * TOPK
        top_i = at(o, BLOCKS, 2, TOPK).bitcast(U32); o += BLOCKS * 2 * TOPK
        top_f, gate_sum = at(o, BLOCKS, 2, TOPK), at(o, NB_P * PH); o += BLOCKS * 2 * TOPK
        cut = at(o, NKEY); o += NKEY
        cand = at(o, TOPK, TOPK); o += TOPK * TOPK
        cand_cut = at(o, TOPK * TOPK); o += TOPK * TOPK
        pick = [at(o + 256 * i, TOPK, TOPK) for i in range(2)]; o += 512
        best_j = at(o, TOPK).bitcast(U32); o += TOPK
        best_ab = [at(o + 2 * TOPK * i, TOPK).bitcast(U32) for i in range(2)]
        best_abf = [at(o + 2 * TOPK * i + TOPK, TOPK) for i in range(2)]; o += 4 * TOPK
        key_f = [at(o + TOPK * i, TOPK) for i in range(2)]; o += 2 * TOPK
        best_s = at(o, TOPK); o += TOPK
        assert o <= MT0
        idx_all = at(V0, BLOCKS, SLOTS).bitcast(I32)
        gate_all = at(V0 + BLOCKS * SLOTS, BLOCKS, SLOTS)
        sub_in = at(V0 + 4 * AW + 512, 2, NKEY)

        u_slot = [at(W0 + D * i, D) for i in range(RING)]
        v_slot = [at(MT0 + D * i, D) for i in range(RING)]
        gate2_p, gate2_s, g_fin = (at(HT0 + D + D * i, D) for i in range(3))
        diag = [at(V0 + 3 * AW + P * i, P) for i in range(GRP)]
        sel = at(V0 + 2 * BLOCKS * SLOTS, NS)
        idx_rep = at(V0 + 2 * BLOCKS * SLOTS + NS, NS).bitcast(I32)
        gate_rep = at(V0 + 2 * BLOCKS * SLOTS + 2 * NS, NS)
        out_buf = at(MT0 + RING * D, 16)

        in_c, in_rows, in_ws, in_wd, in_misc, in_bada = (sem(n) for n in ("in_c", "in_rows", "in_ws", "in_wd", "in_misc", "in_bada"))
        w_loaded = [sem(f"w_loaded{s}") for s in range(2)]
        pool_const = sem("pool_const")
        silu_done = sem("silu_done")
        ada_full, ada_free = sem("ada_full"), sem("ada_free")
        mod_ready, mod_stored = sem("mod_ready"), sem("mod_stored")
        mod_loaded = sem("mod_loaded")
        turn_full = [sem(f"turn_full{i}") for i in range(3)]
        turn_free = [sem(f"turn_free{i}") for i in range(3)]
        x_loaded = [sem(f"x_loaded{i}") for i in range(2)]
        norm_sq, norm_ms, norm_rt, norm_h = sem("norm_sq"), sem("norm_ms"), sem("norm_rt"), sem("norm_h")
        bank_full, bank_free = sem("bank_full"), sem("bank_free")
        ln_var, ln_rt, ln_done = sem("ln_var"), sem("ln_rt"), sem("ln_done")
        tri_done = sem("tri_done")
        sgu_stored = sem("sgu_stored")
        kv_stored = sem("kv_stored")
        dve = sem("dve_step")
        s_full, s_free = sem("s_full"), sem("s_free")
        biased, normed, exped = sem("biased"), sem("normed"), sem("exped")
        o_full, o_free = sem("o_full"), sem("o_free")
        kvk_loaded = [sem(f"kvk_loaded{i}") for i in range(2)]
        kvv_loaded = [sem(f"kvv_loaded{i}") for i in range(2)]
        ss_full, ss_free = sem("ss_full"), sem("ss_free")
        s_biased, s_exped, s_normed = sem("s_biased"), sem("s_exped"), sem("s_normed")
        os_full, os_free = sem("os_full"), sem("os_free")
        q_masked = sem("q_masked")
        x1_loaded, mod2_loaded = sem("x1_loaded"), sem("mod2_loaded")
        x1_done = sem("x1_done")
        qry_full, qry_free = sem("qry_full"), sem("qry_free")
        sc_full, sc_free = sem("sc_full"), sem("sc_free")
        picked, gate_exp = sem("picked"), sem("gate_exp")
        gates_done, rep_loaded, peer_tables = sem("gates_done"), sem("rep_loaded"), sem("peer_tables")
        u_loaded = [sem(f"u_loaded{i}") for i in range(RING)]
        v_loaded = [sem(f"v_loaded{i}") for i in range(RING)]
        u_done, v_done = sem("u_done"), sem("v_done")
        pool_go = sem("pool_go")
        idx_copied = sem("idx_copied")
        gelu_done, coef_done, diag_done = sem("gelu_done"), sem("coef_done"), sem("diag_done")
        zeroed = sem("zeroed")
        fin_x, fin_sq, fin_ms, fin_rt, fin_y, y_stored = (sem(n) for n in ("fin_x", "fin_sq", "fin_ms", "fin_rt", "fin_y", "y_stored"))

        def turn(key):
            return 5 + T[key] % 3, T[key] // 3

        def wait_turn_free(eng, key):
            bank, n = turn(key)
            if n:
                eng.wait_ge(turn_free[bank - 5], n)
            return bank

        def turned(ins, key):
            ins.then_inc(turn_full[turn(key)[0] - 5], 1)

        def wait_turn_full(eng, key):
            bank, n = turn(key)
            eng.wait_ge(turn_full[bank - 5], n + 1)
            return bank

        def turn_read(ins, key):
            ins.then_inc(turn_free[turn(key)[0] - 5], 1)

        def wait_turn_read(eng, key):
            bank, n = turn(key)
            eng.wait_ge(turn_free[bank - 5], n + 1)

        def tok(b):
            return slice(b * P, b * P + ROWS[b])

        IN_ORDER = [8, 9, 6, 7, 0, 1, 2, 3, 4, 5]
        A_USES, IN_USES = ADA_T // 2, IN_T // 2
        T_IN, T_OUT, T_Q = ADA_T, ADA_T + IN_T, ADA_T + IN_T + OUT_T
        w_ada_v = w_ada.rearrange("l (k p) n -> p (l k) n", p=P)
        w_in_v = w_in.rearrange("l (k p) n -> p (l k) n", p=P)
        w_out_v = w_out.rearrange("l (k p) n -> p (l k) n", p=P)
        w_query_v = w_query.rearrange("l (k p) n -> p (l k) n", p=P)

        block = ctx.enter_context(nc.Block())

        @block.sync
        def _(sp):
            sp.dma_start(c_in[0:1, :], c_prompt).then_inc(in_c, 16)
            sp.dma_start(c_in[1:1 + DECB, :], c_sample).then_inc(in_c, 16)

            def tile_used(t):
                if t < T_IN:
                    sp.wait_ge(ada_full, t + 1)
                elif t < T_Q:
                    sp.wait_ge(bank_full, (t - T_IN + 1) * BLOCKS)
                else:
                    sp.wait_ge(qry_full, 2 * (t - T_Q + 1))

            def load_w(t, dst, src):
                if t >= 2:
                    tile_used(t - 2)
                sp.dma_start(dst, src).then_inc(w_loaded[t % 2], 16)

            for n in range(ADA_T):
                load_w(n, w_slot[n % 2], w_ada_v[:, :, n * NC:(n + 1) * NC])
            for i, n in enumerate(IN_ORDER):
                load_w(T_IN + i, w_slot[i % 2], w_in_v[:, :, n * NC:(n + 1) * NC])

            def load_cache(cache, b, dst, s):
                rows = cache.rearrange("l b s h c -> (l b) s (h c)")[b]
                for c in range(FAR):
                    far = bass.AP(rows.tensor, rows.offset + 512 * c * AW, [[16 * AW, 32], [AW, 4], [1, AW]])
                    sp.dma_start(dst[:, c, :], far).then_inc(s, 16)
                near = rows[PAST - 512:PAST, :].rearrange("(c p) n -> p c n", p=P)
                sp.dma_start(dst[:, FAR:CH, :], near).then_inc(s, 16)

            tile_used(T_OUT - 1)
            for b in range(DECB):
                if b == 1:
                    sp.wait_ge(o_full, H)
                    sp.wait_ge(o_free, H)
                    sp.wait_ge(turn_free[turn(("qs",))[0] - 5], turn(("qs",))[1] + 1)
                    sp.wait_ge(kv_stored, 16 * 2 * BLOCKS)
                if b >= 2:
                    sp.wait_ge(os_full, b - 1)
                load_cache(cache_k, b, kv_k[b % 2], kvk_loaded[b % 2])
                load_cache(cache_v, b, kv_v[b % 2], kvv_loaded[b % 2])
            sp.wait_ge(os_full, DECB)
            for n in range(OUT_T):
                load_w(T_OUT + n, w_slot[n % 2], w_out_v[:, :, n * NC:(n + 1) * NC])
            for h in range(PH):
                if h == 0:
                    tile_used(T_Q - 1)
                load_w(T_Q + h, wq_slot[h % 2], w_query_v[:, :, h * 256:(h + 1) * 256])

        @block.gpsimd
        def _(pool):
            steps = [0]

            def step(ins):
                steps[0] += 1
                ins.then_inc(pool_const, 1)
                pool.wait_ge(pool_const, steps[0])

            step(nc.gpsimd.memset(ident, 0.0))
            step(nc.gpsimd.affine_select(out=ident, in_=ident, compare_op=ALU.not_equal, fill=1.0, base=0,
                                         pattern=[[-1, P]], channel_multiplier=1))
            pool.dma_start(mod, b_ada[0].partition_broadcast(1 + DECB)).then_inc(in_bada, 16)
            pool.dma_start(g1_rows, g_norm1[0].partition_broadcast(1 + DECB)).then_inc(in_rows, 16)
            pool.dma_start(g2_rows, g_norm2[0].partition_broadcast(1 + DECB)).then_inc(in_rows, 16)
            step(nc.gpsimd.iota(tmp_i[0][:, 0:SEQ].bitcast(I32), pattern=[[-1, SEQ]], base=SEQ - P, channel_multiplier=1))
            step(nc.gpsimd.iota(tmp_i[1][:, 0:FAR * P].rearrange("p (m r) -> p m r", r=4).bitcast(I32),
                                pattern=[[-16, FAR * 32], [-1, 4]], base=PAST, channel_multiplier=0))
            step(nc.gpsimd.iota(tmp_i[1][:, FAR * P:NK].bitcast(I32), pattern=[[-1, 512]], base=512, channel_multiplier=0))
            step(nc.gpsimd.iota(tmp_i[1][:, NK:NKS].rearrange("p (b t) -> p b t", t=DECT).bitcast(I32),
                                pattern=[[0, DECB], [-1, DECT]], base=0, channel_multiplier=0))
            step(nc.gpsimd.iota(iota_i, pattern=[[1, TOPK]], base=0, channel_multiplier=0))
            step(nc.gpsimd.iota(slope_s.bitcast(I32), pattern=[[0, 1]], base=0, channel_multiplier=1))
            step(nc.gpsimd.memset(bias_new, 0.0))
            v = bias_new.rearrange("p b (k t) -> p b k t", t=DECT)
            step(nc.gpsimd.affine_select(out=v, in_=v, compare_op=ALU.is_equal, fill=NEG, base=0,
                                         pattern=[[1, DECB], [-1, DECB], [0, DECT]], channel_multiplier=0))
            pool.dma_start(ws_in, w_spatial[0].rearrange("g t s -> t g s")).then_inc(in_ws, 16)
            pool.dma_start(ln_g, ln_v_g[0].partition_broadcast(P)).then_inc(in_misc, 16)
            pool.dma_start(ln_b, ln_v_b[0].partition_broadcast(P)).then_inc(in_misc, 16)
            pool.dma_start(bs_p, b_spatial[0].rearrange("g t -> t g"), allow_slow_non_contiguous=True).then_inc(in_misc, 16)
            step(nc.gpsimd.memset(wd_in, 0.0))
            for b in range(DECB):
                r = slice(DECT * b, DECT * b + DECT)
                pool.dma_start(wd_in[r, :, r], w_spatial[0, :, 0:DECT, 0:DECT].rearrange("g t s -> t g s")).then_inc(in_wd, 16)
                pool.dma_start(bs_s[r, :], b_spatial[0, :, 0:DECT].rearrange("g t -> t g"), allow_slow_non_contiguous=True).then_inc(in_misc, 16)
            pool.dma_start(sub_in, sub_keys[0].rearrange("j n c -> n j c")).then_inc(in_misc, 16)
            pool.wait_ge(in_ws, 16)
            nc.gpsimd.affine_select(out=ws_in, in_=ws_in, compare_op=ALU.is_ge, fill=0.0, base=0,
                                    pattern=[[0, G], [-1, P]], channel_multiplier=1).then_inc(tri_done, 1)
            pool.wait_ge(in_wd, 16 * DECB)
            nc.gpsimd.affine_select(out=wd_in, in_=wd_in, compare_op=ALU.is_ge, fill=0.0, base=0,
                                    pattern=[[0, G], [-1, NS]], channel_multiplier=1).then_inc(tri_done, 1)

            pool.wait_ge(mod_ready, 2)
            pool.dma_start(mod_dram, mod).then_inc(mod_stored, 16)
            pool.wait_ge(mod_stored, 16)

            def load_mod(part_of, dst_p, dst_s, s):
                cols = slice(part_of * D, (part_of + 1) * D)
                pool.dma_start(dst_p, mod_dram[0, cols].partition_broadcast(P)).then_inc(s, 16)
                row = mod_dram[1, cols]
                pool.dma_start(dst_s[0:NS, :], bass.AP(row.tensor, row.offset, [[6 * D, DECB], [0, DECT], [1, D]])).then_inc(s, 16)

            load_mod(0, shift1_p, shift1_s, mod_loaded)
            load_mod(1, scale1_p, scale1_s, mod_loaded)
            for b in range(BLOCKS):
                if b >= 2:
                    pool.wait_ge(norm_h, b - 1)
                pool.dma_start(x_buf[b % 2][0:ROWS[b], :], x_of[b]).then_inc(x_loaded[b % 2], 16)

            pool.wait_ge(ln_done, BLOCKS)
            pool.dma_start(sgp, g_all[0:NS, NB_P, :]).then_inc(sgu_stored, 16)
            for i, (src, win, new) in enumerate(((k_all, kwp, knp), (v_all, vwp, vnp))):
                for b in range(BLOCKS):
                    pool.wait_ge(bank_free, BLOCKS + (7 + 2 * i) * BLOCKS + b + 1)
                    dst = win[b * P:(b + 1) * P, :] if b < NB_P else new
                    pool.dma_start(dst, src[0:ROWS[b], b, :]).then_inc(kv_stored, 16)

            pool.wait_ge(os_free, DECB)
            pool.wait_ge(kv_stored, 16 * 2 * BLOCKS)
            for b in range(BLOCKS):
                pool.dma_start(x1[0:ROWS[b], b, :], x_of[b]).then_inc(x1_loaded, 16)
            load_mod(2, gate1_p, gate1_s, mod2_loaded)
            load_mod(3, shift2_p, shift2_s, mod2_loaded)
            load_mod(4, scale2_p, scale2_s, mod2_loaded)

            pool.wait_ge(gates_done, 2)
            load_mod(5, gate2_p, gate2_s, peer_tables)
            pool.dma_start(g_fin, g_final.partition_broadcast(P)).then_inc(peer_tables, 16)
            for q in range(4):
                r = slice(NS * q, NS * q + NS)
                pool.dma_start(idx_rep[r, :], idx_all[0:NS, NB_P, r]).then_inc(rep_loaded, 16)
                pool.dma_start(gate_rep[r, :], gate_all[0:NS, NB_P, r]).then_inc(rep_loaded, 16)
                if q:
                    pool.dma_start(h2[NB_P][r, :], h2[NB_P][0:NS, :]).then_inc(rep_loaded, 16)

            def gather_groups(src, first, i):
                for par in range(2):
                    n = first + par
                    pool.wait_ge(v_done, n * GRP + 1)
                    pool.sem_inc(pool_go, 1)
                    nc.gpsimd.tensor_copy(idx_stage[:, par, :], src[:, bass.ds(i * 2 * GRP + par * GRP, GRP)]).then_inc(idx_copied, 1)
                    pool.wait_ge(idx_copied, n + 1)
                    for table, slots, loaded, done, ahead in (
                            (u_rows, u_slot, u_loaded, u_done, RING), (v_rows, v_slot, v_loaded, v_done, GRP)):
                        for k in range(GRP):
                            pool.wait_ge(done, n * GRP + k + 1 + ahead - RING)
                            pool.sem_inc(pool_go, 1)
                            nc.gpsimd.indirect_dma_start(
                                out=slots[k % RING], out_offset=None, in_=table,
                                in_offset=bass.IndirectOffsetOnAxis(ap=idx_stage[:, par, k:k + 1], axis=0),
                            ).then_inc(loaded[k % RING], 16)

            pool.wait_ge(rep_loaded, 16 * 11)
            pairs = SLOTS // GRP // 2
            for b in range(NB_P):
                with pool.Fori(0, pairs) as i:
                    gather_groups(idx_all[:, b, :], i * 2 + b * 2 * pairs, i)
            with pool.Fori(0, pairs // 4) as i:
                gather_groups(idx_rep, i * 2 + NB_P * 2 * pairs, i)

        @block.scalar
        def _(act):
            act.wait_ge(in_c, 32)
            nc.scalar.activation(c_in, c_in, ACT.Silu).then_inc(silu_done, 1)

            def read_turn(key, dst, shape, rows=P, func=None):
                bank = wait_turn_full(act, key)
                src = ps[0:rows, bank, 0:math.prod(shape)]
                if len(shape) == 2:
                    src = src.rearrange("p (a b) -> p a b", b=shape[1])
                turn_read(nc.scalar.copy(dst, src), key)

            read_turn(("c",), c_t, (KD, 1 + DECB))
            for i in range(2):
                read_turn(("ws", i), ws_t[:, 4 * i:4 * i + 4, :], (4, P))
            read_turn(("wd",), wd_t, (G, NS), rows=NS)
            read_turn(("sk",), sub_t, (2, NKEY))

            def norm_rows(u, x, h, b, wait):
                wait()
                nc.scalar.activation(h[0:ROWS[b], :], x[0:ROWS[b], :], ACT.Square,
                                     accum_out=stat[0:ROWS[b], u:u + 1]).then_inc(norm_sq, 1)
                act.wait_ge(norm_ms, u + 1)
                nc.scalar.activation(stat[0:ROWS[b], u:u + 1], stat[0:ROWS[b], u:u + 1], ACT.Sqrt).then_inc(norm_rt, 1)

            for b in range(BLOCKS):
                def wait(b=b):
                    act.wait_ge(x_loaded[b % 2], 16 * (b // 2 + 1))
                    if b >= 2:
                        wait_turn_full(act, ("h", b - 2, 3))
                norm_rows(b, x_buf[b % 2], h_buf[b % 2], b, wait)
                if b:
                    for g in range(4):
                        read_turn(("h", b - 1, g), h_t[:, 4 * g:4 * g + 4, tok(b - 1)], (4, ROWS[b - 1]))
            for g in range(4):
                read_turn(("h", NB_P, g), h_t[:, 4 * g:4 * g + 4, tok(NB_P)], (4, NS))

            def read_bank(i, b, dst, func):
                act.wait_ge(bank_full, i * BLOCKS + b + 1)
                nc.scalar.activation(dst[0:ROWS[b], b, (i % 2) * NC:(i % 2 + 1) * NC], ps[0:ROWS[b], b, :],
                                     func).then_inc(bank_free, 1)

            for i in range(2):
                for b in range(BLOCKS):
                    read_bank(i, b, g_all, ACT.Gelu)
            for b in range(BLOCKS):
                act.wait_ge(ln_var, b + 1)
                nc.scalar.activation(stat[0:ROWS[b], 10 + b:11 + b], stat[0:ROWS[b], 10 + b:11 + b], ACT.Sqrt).then_inc(ln_rt, 1)
            for i in range(2, 4):
                for b in range(BLOCKS):
                    read_bank(i, b, u_all, ACT.Gelu)
            for b in range(BLOCKS):
                for i in range(2):
                    read_turn(("mt", b, i), mix_t[:, H + 4 * i:H + 4 * i + 4, tok(b)], (4, ROWS[b]))
            for i in range(4, 10):
                if i == 8:
                    act.wait_ge(sgu_stored, 16)
                for b in range(BLOCKS):
                    read_bank(i, b, (q_all, k_all, v_all)[i // 2 - 2], ACT.Copy)

            def turn_heads(h):
                if h >= 2:
                    act.wait_ge(s_full, NB_P * (h - 1))
                read_turn(("q", h), q_t[h % 2], (SEQ,))
                read_turn(("k", h), k_t[h % 2], (SEQ,))

            turn_heads(0)
            for h in range(H):
                if h + 1 < H:
                    turn_heads(h + 1)
                act.wait_ge(biased, h + 1)
                for qi in range(NB_P):
                    nc.scalar.activation(prob[qi], prob[qi], ACT.Exp, bias=stat[:, 32 + qi:33 + qi],
                                         accum_out=stat[:, 36 + qi:37 + qi]).then_inc(exped, 1)
                for j in range(NB_P):
                    if j == 0 and h:
                        act.wait_ge(o_full, h)
                    bank = wait_turn_full(act, ("p", h, j))
                    turn_read(nc.scalar.copy(prob_t[:, j, j * P:SEQ], ps[:, bank, 0:SEQ - j * P]), ("p", h, j))
                act.wait_ge(o_full, h + 1)
                nc.scalar.copy(mix_t[:, h, 0:SEQ], ps[:, 4, :]).then_inc(o_free, 1)

            act.wait_ge(kv_stored, 16 * 2 * BLOCKS)
            read_turn(("qs",), q_st, (H, NS))
            read_turn(("ks",), k_st, (H, NS))
            for b in range(DECB):
                for h in range(0, H):
                    for i in range(2):
                        if i == 0 and b * H + h >= 2:
                            act.wait_ge(ss_full, b * H + h - 1)
                        if (h + i) % 2 == 0:
                            read_turn(("kt", b, h, i), key_t[h % 2][:, 512 * i:min(512 * i + 512, NK)], (min(512, NK - 512 * i),))
                act.wait_ge(s_biased, b + 1)
                nc.scalar.activation(prob_s[b % 2], prob_s[b % 2], ACT.Exp, bias=stat[0:NS, 40:41],
                                     accum_out=stat[0:NS, 41:42]).then_inc(s_exped, 1)
                act.wait_ge(os_full, b + 1)
                nc.scalar.copy(mix_t[:, 0:H, SEQ + DECT * b:SEQ + DECT * b + DECT],
                               ps[:, 3, 0:NS].rearrange("p (h t) -> p h t", t=DECT)).then_inc(os_free, 1)

            for b in range(BLOCKS):
                def wait(b=b):
                    act.wait_ge(x1_done, BLOCKS * OUT_T)
                norm_rows(BLOCKS + b, x1[:, b, :], h2[b], b, wait)
                if b:
                    for g in range(4):
                        read_turn(("h2", b - 1, g), h2_t[:, 4 * g:4 * g + 4, tok(b - 1)], (4, ROWS[b - 1]))
            for g in range(4):
                read_turn(("h2", NB_P, g), h2_t[:, 4 * g:4 * g + 4, tok(NB_P)], (4, NS))

            with act.Fori(0, PH) as h:
                for j in range(2):
                    act.wait_ge(qry_full, h * 2 + j + 1)
                    nc.scalar.copy(qry_t[j][:, 0:SEQ], ps[:, 2 * j, :]).then_inc(qry_free, 1)
                    nc.scalar.copy(qry_t[j][:, SEQ:NTOK], ps[:, 2 * j + 1, 0:NS]).then_inc(qry_free, 1)

            act.wait_ge(gates_done, 1)
            g_flat = gate_all.rearrange("p b s -> p (b s)")
            nc.scalar.activation(g_flat[:, 0:NB_P * SLOTS], g_flat[:, 0:NB_P * SLOTS], ACT.Exp).then_inc(gate_exp, 1)
            nc.scalar.activation(g_flat[0:NS, NB_P * SLOTS:], g_flat[0:NS, NB_P * SLOTS:], ACT.Exp).then_inc(gate_exp, 1)

            def groups(n0):
                for par in range(2):
                    n = n0 + par
                    act.wait_ge(u_done, n * GRP + GRP + RING)
                    nc.scalar.activation(act_gelu[:, par, :], act_sum[:, par, :], ACT.Gelu).then_inc(gelu_done, 1)
                    act.wait_ge(coef_done, n + 1)
                    for k in range(GRP):
                        act.wait_ge(v_done, n * GRP + k + 1)
                        if is_sample[0]:
                            nc.scalar.activation(diag[k][:, 0:NS], sel, ACT.Copy, scale=coef[:, par, k:k + 1]).then_inc(diag_done, 1)
                        else:
                            nc.scalar.activation(diag[k], ident, ACT.Copy, scale=coef[:, par, k:k + 1]).then_inc(diag_done, 1)

            def finish(b):
                r = ROWS[b]
                act.wait_ge(fin_x, b + 1)
                bank = 4 * (b % 2)
                nc.scalar.activation(ps[0:r, bank:bank + 4, :].rearrange("p a n -> p (a n)"), x1[0:r, b, :], ACT.Square,
                                     accum_out=stat[0:r, 48 + b:49 + b]).then_inc(fin_sq, 1)
                act.wait_ge(fin_ms, b + 1)
                nc.scalar.activation(stat[0:r, 48 + b:49 + b], stat[0:r, 48 + b:49 + b], ACT.Sqrt).then_inc(fin_rt, 1)
                act.wait_ge(fin_y, b + 1)
                act.dma_start(y_of[b], x1[0:r, b, :]).then_inc(y_stored, 16)

            is_sample = [False]
            pairs = SLOTS // GRP // 2
            for b in range(BLOCKS):
                is_sample[0] = b == NB_P
                base = b * 2 * pairs
                groups(base)
                if b:
                    finish(b - 1)
                with act.Fori(1, pairs if b < NB_P else pairs // 4) as i:
                    groups(i * 2 + base)
            finish(NB_P)
            act.wait_ge(y_stored, 16 * BLOCKS)
            act.wait_ge(sgu_stored, 16)
            act.wait_ge(kv_stored, 16 * 2 * BLOCKS)

        @block.vector
        def _(dv):
            chain = [0]
            V = nc.vector

            def link(ins):
                chain[0] += 1
                ins.then_inc(dve, 1)
                dv.wait_ge(dve, chain[0])

            dv.sem_inc(u_done, RING)
            dv.wait_ge(pool_const, 10)

            def branch_counts(di, df, c, t, ti, n, rows):
                di, df, c, t, ti = di[0:rows, 0:n], df[0:rows, 0:n], c[0:rows, 0:n], t[0:rows, 0:n], ti[0:rows, 0:n]
                link(V.tensor_scalar(c, df, float(WINDOWS[0][0]), None, ALU.is_le))
                for window, dil in WINDOWS[1:]:
                    link(V.tensor_scalar(ti.bitcast(I32), di.bitcast(I32), dil - 1, None, ALU.bitwise_and))
                    link(V.tensor_scalar(t, ti.bitcast(I32), 0.0, None, ALU.is_equal))
                    link(V.scalar_tensor_tensor(out=t, in0=df, scalar=float(window), in1=t, op0=ALU.is_le, op1=ALU.mult))
                    link(V.tensor_tensor(c, c, t, ALU.add))
                link(V.scalar_tensor_tensor(out=c, in0=df, scalar=0.0, in1=c, op0=ALU.is_ge, op1=ALU.mult))
                link(V.tensor_scalar(t, c, 0.0, NEG, ALU.is_equal, ALU.mult))
                link(V.tensor_scalar(ti, c, 2.0, math.log(2.0), ALU.is_equal, ALU.mult))
                link(V.tensor_tensor(t, t, ti, ALU.add))
                link(V.tensor_scalar(ti, c, 3.0, math.log(3.0), ALU.is_equal, ALU.mult))
                link(V.tensor_tensor(c, t, ti, ALU.add))

            link(V.tensor_copy(delta, tmp_i[0][:, 0:SEQ].bitcast(I32)))
            branch_counts(tmp_i[0], delta, count_ln, tmp_i[2], tmp_i[3], SEQ, P)
            row, head = stat[0:NS, 60:61], stat[0:NS, 61:62]
            dist_s = tmp_i[0][0:NS, 0:NKS]
            link(V.tensor_scalar(row.bitcast(I32), slope_s.bitcast(I32), DECT - 1, None, ALU.bitwise_and))
            link(V.tensor_scalar(head.bitcast(I32), slope_s.bitcast(I32), 2, None, ALU.logical_shift_right))
            link(V.tensor_copy(stat[0:NS, 62:63], row.bitcast(I32)))
            link(V.tensor_copy(stat[0:NS, 63:64], head.bitcast(I32)))
            link(V.tensor_scalar(dist_s, tmp_i[1][0:NS, 0:NKS].bitcast(I32), stat[0:NS, 62:63], None, ALU.add))
            link(V.tensor_copy(tmp_i[1][0:NS, 0:NKS].bitcast(I32), dist_s))
            link(V.tensor_copy(iota16, iota_i))
            link(V.tensor_scalar(slope_s.bitcast(I32), stat[0:NS, 63:64], -float(1 << 23), float(126 << 23), ALU.mult, ALU.add))
            branch_counts(tmp_i[1], dist_s, bias_s, tmp_i[2], tmp_i[3], NKS, NS)
            link(V.tensor_scalar(tmp_i[2][0:NS, 0:NKS], dist_s, slope_s, -1.0, ALU.mult, ALU.mult))
            link(V.tensor_tensor(bias_s, bias_s, tmp_i[2][0:NS, 0:NKS], ALU.add))
            link(V.tensor_tensor(bias_new, bias_new, bias_s[:, NK:NKS].unsqueeze(1).broadcast_to([NS, DECB, NS]), ALU.add))

            dv.wait_ge(in_bada, 16)
            with dv.Fori(0, ADA_T // 2) as i:
                for s in range(2):
                    dv.wait_ge(ada_full, i * 2 + s + 1)
                    m = mod[:, bass.ds((i * 2 + s) * NC, NC)]
                    V.tensor_tensor(m, ps[0:1 + DECB, s, :], m, ALU.add).then_inc(ada_free, 1)
            dv.wait_ge(ada_free, 2 + ADA_T)
            dv.wait_ge(in_rows, 32)
            for j, gain in ((1, g1_rows), (4, g2_rows)):
                m = mod[:, j * D:(j + 1) * D]
                V.scalar_tensor_tensor(out=m, in0=m, scalar=1.0, in1=gain, op0=ALU.add, op1=ALU.mult).then_inc(mod_ready, 1)

            def norm(u, x, h, b, scale, shift):
                r = ROWS[b]
                x, h, scale, shift = x[0:r, :], h[0:r, :], scale[0:r, :], shift[0:r, :]
                s = stat[0:r, u:u + 1]
                dv.wait_ge(norm_sq, u + 1)
                V.tensor_scalar(s, s, 1.0 / D, EPS, ALU.mult, ALU.add).then_inc(norm_ms, 1)
                dv.wait_ge(norm_rt, u + 1)
                link(V.reciprocal(s, s))
                link(V.scalar_tensor_tensor(out=h, in0=x, scalar=s, in1=scale, op0=ALU.mult, op1=ALU.mult))
                V.tensor_tensor(h, h, shift, ALU.add).then_inc(norm_h, 1)

            dv.wait_ge(mod_loaded, 64)
            for b in range(BLOCKS):
                norm(b, x_buf[b % 2], h_buf[b % 2], b, *((scale1_p, shift1_p) if b < NB_P else (scale1_s, shift1_s)))

            dv.wait_ge(in_misc, 16 * (3 + DECB + 1))
            for b in range(BLOCKS):
                r = ROWS[b]
                g = g_all[0:r, b, :]
                st, mv, sd = stat[0:r, 20:32], stat[0:r, 44:46], stat[0:r, 10 + b:11 + b]
                dv.wait_ge(bank_free, BLOCKS + BLOCKS + b + 1)
                for i in range(2):
                    link(V.bn_stats(out=st[:, 6 * i:6 * i + 6], in_=g[:, i * NC:(i + 1) * NC]))
                link(V.bn_aggr(out=mv, in_=st))
                V.tensor_scalar(sd, mv[:, 1:2], EPS, None, ALU.add).then_inc(ln_var, 1)
                dv.wait_ge(ln_rt, b + 1)
                link(V.reciprocal(sd, sd))
                link(V.tensor_scalar(g, g, mv[:, 0:1], sd, ALU.subtract, ALU.mult))
                link(V.tensor_tensor(g, g, ln_g[0:r, :], ALU.mult))
                V.tensor_tensor(g, g, ln_b[0:r, :], ALU.add).then_inc(ln_done, 1)
            dv.wait_ge(bank_free, BLOCKS + 4 * BLOCKS)
            for b in range(BLOCKS):
                r = ROWS[b]
                bs = bs_p if b < NB_P else bs_s
                for i in range(2):
                    bank = wait_turn_full(dv, ("m", b, i))
                    for g in range(4):
                        cols = slice((4 * i + g) * P, (4 * i + g + 1) * P)
                        ins = V.scalar_tensor_tensor(out=u_all[0:r, b, cols], in0=ps[0:r, bank, g * P:(g + 1) * P],
                                                     scalar=bs[0:r, 4 * i + g:4 * i + g + 1], in1=u_all[0:r, b, cols],
                                                     op0=ALU.add, op1=ALU.mult)
                    turn_read(ins, ("m", b, i))

            dv.wait_ge(bank_full, IN_T * BLOCKS)
            for h in range(H):
                link(V.scalar_tensor_tensor(out=head_bias, in0=delta, scalar=-2.0 ** -(h + 1), in1=count_ln,
                                            op0=ALU.mult, op1=ALU.add))
                for qi in range(NB_P):
                    dv.wait_ge(s_full, NB_P * h + qi + 1)
                    if h and qi == 0:
                        for j in range(NB_P):
                            bank, n = turn(("p", h - 1, j))
                            dv.wait_ge(turn_full[bank - 5], n + 1)
                    n = (qi + 1) * P
                    V.scalar_tensor_tensor(out=prob[qi], in0=ps[:, qi, 0:n], scalar=SCALE, in1=head_bias[:, SEQ - n:SEQ],
                                           op0=ALU.mult, op1=ALU.add).then_inc(s_free, 1)
                    dv.wait_ge(s_free, NB_P * h + qi + 1)
                    link(V.reduce_max(stat[:, 32 + qi:33 + qi], prob[qi], AX_X))
                V.tensor_scalar(stat[:, 32:36], stat[:, 32:36], -1.0, None, ALU.mult).then_inc(biased, 1)
                dv.wait_ge(exped, NB_P * (h + 1))
                link(V.reciprocal(stat[:, 36:40], stat[:, 36:40]))
                for qi in range(NB_P):
                    V.tensor_scalar(prob[qi], prob[qi], stat[:, 36 + qi:37 + qi], None, ALU.mult).then_inc(normed, 1)
                dv.wait_ge(normed, NB_P * (h + 1))

            dv.wait_ge(o_full, H)
            dv.wait_ge(kv_stored, 16 * 2 * BLOCKS)
            for par in range(2):
                link(V.memset(q_mask[par], 0.0))
            bank, n = turn(("qs",))
            dv.wait_ge(turn_free[bank - 5], n + 1)
            for b in range(DECB):
                if b >= 2:
                    dv.wait_ge(ss_full, H * (b - 1))
                m = q_mask[b % 2]
                own = bass.AP(m.tensor, m.offset, [m.ap[0], [NS + DECT, H], [1, DECT]])
                V.tensor_copy(own, q_st[:, :, DECT * b:DECT * b + DECT]).then_inc(q_masked, 1)
                for h in range(H):
                    for i in range(2):
                        if i == 0 and b * H + h >= 2:
                            dv.wait_ge(ss_full, b * H + h - 1)
                        if (h + i) % 2 == 1:
                            key = ("kt", b, h, i)
                            n = min(512, NK - 512 * i)
                            bank = wait_turn_full(dv, key)
                            turn_read(V.tensor_copy(key_t[h % 2][:, 512 * i:512 * i + n], ps[:, bank, 0:n]), key)
                p = prob_s[b % 2]
                dv.wait_ge(ss_full, H * (b + 1))
                if b >= 2:
                    dv.wait_ge(os_full, b - 1)
                for j, (lo, n) in enumerate(((0, 512), (512, NK - 512))):
                    link(V.scalar_tensor_tensor(out=p[:, lo:lo + n], in0=ps[0:NS, j, 0:n], scalar=SCALE,
                                                in1=bias_s[:, lo:lo + n], op0=ALU.mult, op1=ALU.add))
                V.scalar_tensor_tensor(out=p[:, NK:NKS], in0=ps[0:NS, 2, 0:NS], scalar=SCALE, in1=bias_new[:, b, :],
                                       op0=ALU.mult, op1=ALU.add).then_inc(ss_free, 1)
                dv.wait_ge(ss_free, b + 1)
                link(V.reduce_max(stat[0:NS, 40:41], p, AX_X))
                V.tensor_scalar(stat[0:NS, 40:41], stat[0:NS, 40:41], -1.0, None, ALU.mult).then_inc(s_biased, 1)
                dv.wait_ge(s_exped, b + 1)
                link(V.reciprocal(stat[0:NS, 41:42], stat[0:NS, 41:42]))
                V.tensor_scalar(p, p, stat[0:NS, 41:42], None, ALU.mult).then_inc(s_normed, 1)
                key = ("pt", b)
                bank = wait_turn_full(dv, key)
                link(V.tensor_copy(prob_st[b % 2][:, 0:CH, :], ps[:, bank, 0:CH * NS].rearrange("p (c n) -> p c n", n=NS)))
                turn_read(V.tensor_copy(prob_st[b % 2][0:NS, CH, :], ps[0:NS, bank, CH * NS:(CH + 1) * NS]), key)

            dv.wait_ge(x1_loaded, 16 * BLOCKS)
            dv.wait_ge(mod2_loaded, 16 * 6)
            for n in range(OUT_T):
                for b in range(BLOCKS):
                    r = ROWS[b]
                    e = n * BLOCKS + b
                    cols = slice(n * NC, (n + 1) * NC)
                    gate = gate1_p if b < NB_P else gate1_s
                    pt = part[e % 2][0:r, :]
                    dv.wait_ge(bank_full, (IN_T + n) * BLOCKS + b + 1)
                    if e >= 2:
                        dv.wait_ge(x1_done, e - 1)
                    V.tensor_tensor(pt, ps[0:r, b, :], gate[0:r, cols], ALU.mult).then_inc(bank_free, 1)
                    dv.wait_ge(bank_free, BLOCKS + IN_T * BLOCKS + e + 1)
                    V.tensor_tensor(x1[0:r, b, cols], x1[0:r, b, cols], pt, ALU.add).then_inc(x1_done, 1)
            for b in range(BLOCKS):
                norm(BLOCKS + b, x1[:, b, :], h2[b], b, *((scale2_p, shift2_p) if b < NB_P else (scale2_s, shift2_s)))

            dv.wait_ge(norm_h, 2 * BLOCKS)
            for h in range(PH):
                def top16(values, scratch, out_s, out_i):
                    link(V.max(out_s[:, 0:8], values))
                    link(V.max_index(out_i[:, 0:8], out_s[:, 0:8], values))
                    link(V.match_replace(scratch, out_s[:, 0:8], values, -3.0e38))
                    link(V.max(out_s[:, 8:16], scratch))
                    link(V.max_index(out_i[:, 8:16], out_s[:, 8:16], scratch))

                for j in range(2):
                    dv.wait_ge(sc_full, h * 2 + j + 1)
                    for b in range(BLOCKS):
                        r = ROWS[b]
                        sc = ps[0:r, 4 + 2 * j, b * NKEY:(b + 1) * NKEY] if b < NB_P else ps[0:r, 5 + 2 * j, 0:NKEY]
                        top16(sc, cut[0:r, :], top_s[0:r, b, j, :], top_i[0:r, b, j, :])
                    V.sem_inc(sc_free, 1)
                for b in range(BLOCKS):
                    r = ROWS[b]
                    cols = slice(h * TOPK, (h + 1) * TOPK)
                    link(V.tensor_copy(top_f[0:r, b, :, :], top_i[0:r, b, :, :]))
                    shape = [r, TOPK, TOPK]
                    link(V.tensor_tensor(cand[0:r], top_s[0:r, b, 0, :].unsqueeze(2).broadcast_to(shape),
                                          top_s[0:r, b, 1, :].unsqueeze(1).broadcast_to(shape), ALU.add))
                    best = best_s[0:r, :]
                    top16(cand[0:r].rearrange("p a b -> p (a b)"), cand_cut[0:r, :], best, best_j[0:r, :])
                    link(V.tensor_scalar(gate_all[0:r, b, cols], best, best[:, 0:1], None, ALU.subtract))
                    link(V.tensor_scalar(best_ab[0][0:r], best_j[0:r], 4, None, ALU.logical_shift_right))
                    link(V.tensor_scalar(best_ab[1][0:r], best_j[0:r], TOPK - 1, None, ALU.bitwise_and))
                    for j in range(2):
                        link(V.tensor_copy(best_abf[j][0:r], best_ab[j][0:r]))
                        link(V.tensor_tensor(pick[j][0:r], best_abf[j][0:r, :].unsqueeze(2).broadcast_to(shape),
                                              iota16[0:r, :].unsqueeze(1).broadcast_to(shape), ALU.is_equal))
                        link(V.tensor_tensor(pick[j][0:r], pick[j][0:r], top_f[0:r, b, j, :].unsqueeze(1).broadcast_to(shape), ALU.mult))
                        link(V.reduce_sum(key_f[j][0:r, :], pick[j][0:r], AX_X))
                    link(V.scalar_tensor_tensor(out=idx_all[0:r, b, cols], in0=key_f[0][0:r, :], scalar=float(NKEY),
                                                 in1=key_f[1][0:r, :], op0=ALU.mult, op1=ALU.add))
            dv.sem_inc(gates_done, 1)

            dv.wait_ge(gate_exp, 2)
            for r, lo, n in ((P, 0, NB_P), (NS, NB_P, 1)):
                g = gate_all[0:r, lo:lo + n, :].rearrange("p b (h k) -> p (b h) k", k=TOPK)
                s = gate_sum[0:r, 0:n * PH]
                link(V.reduce_sum(s, g, AX_X))
                link(V.reciprocal(s, s))
                link(V.tensor_tensor(g, g, s.unsqueeze(2).broadcast_to([r, n * PH, TOPK]), ALU.mult))
            for q in range(4):
                r = slice(NS * q, NS * q + NS)
                link(V.tensor_copy(sel[r, :], ident[r, r]))
            for half in range(2):
                V.memset(ps[:, 4 * half:4 * half + 4, :].rearrange("p a n -> p (a n)"), 0.0).then_inc(zeroed, 1)
            dv.wait_ge(zeroed, 2)
            dv.sem_inc(gates_done, 1)

            def groups(h_rows, gates, n0, i):
                for par in range(2):
                    n = n0 + par
                    for k in range(GRP):
                        dv.wait_ge(u_loaded[k % RING], (n * 2 + k // RING + 1) * 16)
                        V.tensor_tensor_reduce(out=u_slot[k % RING], in0=u_slot[k % RING], in1=h_rows, scale=1.0, scalar=0.0,
                                               op0=ALU.mult, op1=ALU.add, accum_out=act_sum[:, par, k:k + 1]).then_inc(u_done, 1)
                    dv.wait_ge(gelu_done, n + 1)
                    V.tensor_tensor(coef[:, par, :], act_gelu[:, par, :], gates[:, bass.ds(i * 2 * GRP + par * GRP, GRP)],
                                    ALU.mult).then_inc(coef_done, 1)

            def finish(b):
                r = ROWS[b]
                total = GRP * (1 + (2 * (SLOTS // GRP // 2) * (b + 1) if b < NB_P else 2 * (SLOTS // GRP // 2) * NB_P + 4))
                gate = gate2_p if b < NB_P else gate2_s
                bank = 4 * (b % 2)
                acc = ps[0:r, bank:bank + 4, :].rearrange("p a n -> p (a n)")
                dv.wait_ge(v_done, total)
                link(V.tensor_tensor(acc, acc, gate[0:r, :], ALU.mult))
                V.tensor_tensor(x1[0:r, b, :], x1[0:r, b, :], acc, ALU.add).then_inc(fin_x, 1)
                dv.wait_ge(fin_sq, b + 1)
                if b + 2 < BLOCKS:
                    V.memset(ps[:, bank:bank + 4, :].rearrange("p a n -> p (a n)"), 0.0).then_inc(zeroed, 1)
                s = stat[0:r, 48 + b:49 + b]
                V.tensor_scalar(s, s, 1.0 / D, EPS, ALU.mult, ALU.add).then_inc(fin_ms, 1)
                dv.wait_ge(fin_rt, b + 1)
                link(V.reciprocal(s, s))
                V.scalar_tensor_tensor(out=x1[0:r, b, :], in0=x1[0:r, b, :], scalar=s, in1=g_fin[0:r, :],
                                       op0=ALU.mult, op1=ALU.mult).then_inc(fin_y, 1)

            dv.wait_ge(rep_loaded, 16 * 11)
            dv.wait_ge(peer_tables, 16 * 3)
            pairs = SLOTS // GRP // 2
            for b in range(BLOCKS):
                base = b * 2 * pairs
                gates = gate_all[:, b, :] if b < NB_P else gate_rep
                groups(h2[b], gates, base, 0)
                if b:
                    finish(b - 1)
                with dv.Fori(1, pairs if b < NB_P else pairs // 4) as i:
                    groups(h2[b], gates, i * 2 + base, i)
            finish(NB_P)

        @block.tensor
        def _(pe):
            TT, MM = nc.tensor.transpose, nc.tensor.matmul
            pe.sem_inc(bank_free, BLOCKS)
            pe.sem_inc(ada_free, 2)
            pe.sem_inc(v_done, GRP)

            def turn_many(key, pieces):
                bank = wait_turn_free(pe, key)
                at_col = 0
                for src, rows, cols in pieces:
                    ins = TT(ps[0:cols, bank, at_col:at_col + rows], src, ident[0:rows, 0:rows])
                    at_col += rows
                turned(ins, key)

            pe.wait_ge(pool_const, 2)
            pe.wait_ge(silu_done, 1)
            turn_many(("c",), [(c_in[:, k * P:(k + 1) * P], 1 + DECB, P) for k in range(KD)])
            pe.wait_ge(tri_done, 2)
            for i in range(2):
                turn_many(("ws", i), [(ws_in[:, 4 * i + g, :], P, P) for g in range(4)])
            turn_many(("wd",), [(wd_in[:, g, :], NS, NS) for g in range(G)])
            pe.wait_ge(in_misc, 16 * (3 + DECB + 1))
            turn_many(("sk",), [(sub_in[:, j, :], P, P) for j in range(2)])

            bank, n = turn(("c",))
            pe.wait_ge(turn_free[bank - 5], n + 1)
            with pe.Fori(0, ADA_T // 2) as i:
                for s in range(2):
                    pe.wait_ge(w_loaded[s], (i + 1) * 16)
                    pe.wait_ge(ada_free, i * 2 + s + 1)
                    for k in range(KD):
                        ins = MM(ps[0:1 + DECB, s, :], c_t[:, k, :], w_slot[s][:, k, :], start=(k == 0), stop=(k == KD - 1))
                        if k == KD - 1:
                            ins.then_inc(ada_full, 1)
            pe.wait_ge(ada_free, 2 + ADA_T)

            for b in range(BLOCKS):
                pe.wait_ge(norm_h, b + 1)
                for g in range(4):
                    turn_many(("h", b, g), [(h_buf[b % 2][0:ROWS[b], (4 * g + k) * P:(4 * g + k + 1) * P], ROWS[b], P) for k in range(4)])

            def project(lhs, first, uses, pairs, tile0):
                with pe.Fori(0, pairs) as i:
                    for s in range(2):
                        pe.wait_ge(w_loaded[s], (i + uses + 1) * 16)
                        for b in range(BLOCKS):
                            pe.wait_ge(bank_free, (i * 2 + first + s) * BLOCKS + b + 1)
                            for k in range(KD):
                                ins = MM(ps[0:ROWS[b], b, :], lhs[:, k, tok(b)], w_slot[s][:, k, :],
                                         start=(k == 0), stop=(k == KD - 1))
                            ins.then_inc(bank_full, 1)

            for key in [("h", NB_P, g) for g in range(4)]:
                bank, n = turn(key)
                pe.wait_ge(turn_free[bank - 5], n + 1)
            project(h_t, 0, A_USES, 2, T_IN)
            for b in range(BLOCKS):
                pe.wait_ge(ln_done, b + 1)
                r = ROWS[b]
                for i in range(2):
                    key = ("m", b, i)
                    bank = wait_turn_free(pe, key)
                    for g in range(4):
                        w = ws_t if b < NB_P else wd_t
                        ins = MM(ps[0:r, bank, g * P:(g + 1) * P], w[0:r, 4 * i + g, 0:r],
                                 g_all[0:r, b, (4 * i + g) * P:(4 * i + g + 1) * P], start=True, stop=True)
                    turned(ins, key)
            for b in range(BLOCKS):
                wait_turn_read(pe, ("m", b, 1))
                for i in range(2):
                    turn_many(("mt", b, i), [(u_all[0:ROWS[b], b, (4 * i + g) * P:(4 * i + g + 1) * P], ROWS[b], P) for g in range(4)])
            project(h_t, 4, A_USES + 2, 3, T_IN + 4)

            pe.wait_ge(bank_free, BLOCKS + IN_T * BLOCKS)

            def scores(h):
                cols = slice(h * DH, (h + 1) * DH)
                turn_many(("q", h), [(q_all[:, b, cols], P, P) for b in range(NB_P)])
                turn_many(("k", h), [(k_all[:, b, cols], P, P) for b in range(NB_P)])
                for key in (("q", h), ("k", h)):
                    bank, n = turn(key)
                    pe.wait_ge(turn_free[bank - 5], n + 1)
                for qi in range(NB_P):
                    if h:
                        pe.wait_ge(s_free, NB_P * (h - 1) + qi + 1)
                    MM(ps[:, qi, 0:(qi + 1) * P], q_t[h % 2][:, qi * P:(qi + 1) * P], k_t[h % 2][:, 0:(qi + 1) * P],
                       start=True, stop=True).then_inc(s_full, 1)

            scores(0)
            for h in range(H):
                if h + 1 < H:
                    scores(h + 1)
                pe.wait_ge(normed, NB_P * (h + 1))
                for j in range(NB_P):
                    turn_many(("p", h, j), [(prob[qi][:, j * P:(j + 1) * P], P, P) for qi in range(j, NB_P)])
                if h:
                    pe.wait_ge(o_free, h)
                for j in range(NB_P):
                    bank, n = turn(("p", h, j))
                    pe.wait_ge(turn_free[bank - 5], n + 1)
                    ins = MM(ps[:, 4, j * P:SEQ], v_all[:, j, h * DH:(h + 1) * DH], prob_t[:, j, j * P:SEQ],
                             start=(j == 0), stop=(j == NB_P - 1))
                ins.then_inc(o_full, 1)

            pe.wait_ge(s_free, NB_P * H)
            turn_many(("qs",), [(q_all[0:NS, NB_P, h * DH:(h + 1) * DH], NS, P) for h in range(H)])
            turn_many(("ks",), [(k_all[0:NS, NB_P, h * DH:(h + 1) * DH], NS, P) for h in range(H)])
            bank, n = turn(("ks",))
            pe.wait_ge(turn_free[bank - 5], n + 1)
            for b in range(DECB):
                pe.wait_ge(q_masked, b + 1)
                pe.wait_ge(kvk_loaded[b % 2], 64 * (b // 2 + 1))
                keys, vals = kv_k[b % 2], kv_v[b % 2]

                def turn_keys(h):
                    cols = slice(h * DH, (h + 1) * DH)
                    turn_many(("kt", b, h, 0), [(keys[:, c, cols], P, P) for c in range(4)])
                    turn_many(("kt", b, h, 1), [(keys[:, c, cols], P, P) for c in range(4, CH)])

                turn_keys(0)
                for h in range(H):
                    if h + 1 < H:
                        turn_keys(h + 1)
                    for i in range(2):
                        bank, n = turn(("kt", b, h, i))
                        pe.wait_ge(turn_free[bank - 5], n + 1)
                    if b and h == 0:
                        pe.wait_ge(ss_free, b)
                    q = q_mask[b % 2][:, h, :]
                    MM(ps[0:NS, 0, :], q, key_t[h % 2][:, 0:512], start=(h == 0), stop=(h == H - 1))
                    MM(ps[0:NS, 1, 0:NK - 512], q, key_t[h % 2][:, 512:NK], start=(h == 0), stop=(h == H - 1))
                    MM(ps[0:NS, 2, 0:NS], q, k_st[:, h, :], start=(h == 0), stop=(h == H - 1)).then_inc(ss_full, 1)
                pe.wait_ge(s_normed, b + 1)
                turn_many(("pt", b), [(prob_s[b % 2][:, c * P:min((c + 1) * P, NKS)], NS, min(P, NKS - c * P)) for c in range(CH + 1)])
                bank, n = turn(("pt", b))
                pe.wait_ge(turn_free[bank - 5], n + 1)
                pe.wait_ge(kvv_loaded[b % 2], 64 * (b // 2 + 1))
                if b:
                    pe.wait_ge(os_free, b)
                for h in range(H):
                    cols = slice(h * DH, (h + 1) * DH)
                    out = ps[:, 3, DECT * h:DECT * h + DECT]
                    for c in range(CH):
                        MM(out, vals[:, c, cols], prob_st[b % 2][:, c, DECT * h:DECT * h + DECT], start=(c == 0), stop=False)
                    ins = MM(out, v_all[0:NS, NB_P, cols], prob_st[b % 2][0:NS, CH, DECT * h:DECT * h + DECT], start=False, stop=True)
                ins.then_inc(os_full, 1)

            pe.wait_ge(os_free, DECB)
            pe.wait_ge(o_free, H)
            project(mix_t, IN_T, A_USES + IN_USES, OUT_T // 2, T_OUT)
            for b in range(BLOCKS):
                pe.wait_ge(norm_h, BLOCKS + b + 1)
                for g in range(4):
                    turn_many(("h2", b, g), [(h2[b][0:ROWS[b], (4 * g + k) * P:(4 * g + k + 1) * P], ROWS[b], P) for k in range(4)])
            for g in range(4):
                bank, n = turn(("h2", NB_P, g))
                pe.wait_ge(turn_free[bank - 5], n + 1)
            pe.wait_ge(bank_free, BLOCKS + (IN_T + OUT_T) * BLOCKS)

            pe.sem_inc(qry_free, 4)
            pe.sem_inc(sc_free, 2)
            with pe.Fori(0, PH // 2) as i:
                for s in range(2):
                    pe.wait_ge(w_loaded[s], (i + A_USES + IN_USES + OUT_T // 2 + 1) * 16)
                    for j in range(2):
                        hp = i * 4 + (2 * s + j)
                        pe.wait_ge(qry_free, hp * 2 + 2)
                        for k in range(KD):
                            w = wq_slot[s][:, k, j * P:(j + 1) * P]
                            MM(ps[:, 2 * j, :], w, h2_t[:, k, 0:SEQ], start=(k == 0), stop=(k == KD - 1))
                            ins = MM(ps[:, 2 * j + 1, 0:NS], w, h2_t[:, k, SEQ:NTOK], start=(k == 0), stop=(k == KD - 1))
                        ins.then_inc(qry_full, 1)
                        pe.wait_ge(qry_free, hp * 2 + 6)
                        pe.wait_ge(sc_free, hp + 1)
                        for b in range(BLOCKS):
                            out = ps[0:ROWS[b], 4 + 2 * j, b * NKEY:(b + 1) * NKEY] if b < NB_P else ps[0:NS, 5 + 2 * j, 0:NKEY]
                            ins = MM(out, qry_t[j][:, tok(b)], sub_t[:, j, :], start=True, stop=True)
                        ins.then_inc(sc_full, 1)

            def groups(n0, bank, rows):
                for par in range(2):
                    n = n0 + par
                    for k in range(GRP):
                        pe.wait_ge(diag_done, n * GRP + k + 1)
                        pe.wait_ge(v_loaded[k % RING], (n * 2 + k // RING + 1) * 16)
                        for c in range(4):
                            ins = MM(ps[0:rows, bank + c, :], diag[k][:, 0:rows], v_slot[k % RING][:, c * NC:(c + 1) * NC],
                                     start=False, stop=False, skip_group_check=True)
                        ins.then_inc(v_done, 1)

            pairs = SLOTS // GRP // 2
            for b in range(BLOCKS):
                pe.wait_ge(zeroed, 2 if b < 2 else b + 1)
                with pe.Fori(0, pairs if b < NB_P else pairs // 4) as i:
                    groups(i * 2 + b * 2 * pairs, 4 * (b % 2), ROWS[b])


_INS = ["x_prompt", "x_sample", "cache_k", "cache_v", "c_prompt", "c_sample", "w_ada", "b_ada", "g_norm1", "w_in",
        "ln_v_g", "ln_v_b", "w_spatial", "b_spatial", "w_out", "g_norm2", "w_query", "sub_keys", "expert_u",
        "expert_v", "g_final"]
_OUTS = [(1, SEQ, D), (DECB, DECT, D), (1, 1, SEQ, H, DH), (1, 1, SEQ, H, DH), (1, DECB, DECT, H, DH),
         (1, DECB, DECT, H, DH), (1, DECB, DECT, AW)]


def kernel(**inputs):
    import numpy as _np
    import concourse.bacc as _bacc
    from concourse.bass_utils import run_bass_kernel_spmd as _run

    nc = _bacc.Bacc("TRN2", target_bir_lowering=False, num_devices=1)
    arrays, args = {}, []
    for name in _INS:
        a = _np.ascontiguousarray(inputs[name])
        arrays[f"in_{name}_dram"] = a
        args.append(nc.dram_tensor(f"in_{name}_dram", a.shape, mybir.dt.from_np(a.dtype), kind="ExternalInput").ap())
    for i, shape in enumerate(_OUTS):
        args.append(nc.dram_tensor(f"out_{i}_dram", shape, F32, kind="ExternalOutput").ap())
    trunk_step(nc, *args)
    r = _run(nc, [arrays], core_ids=[0])
    return tuple(r.results[0][f"out_{i}_dram"] for i in range(len(_OUTS)))
```

```python
import math
from contextlib import ExitStack

import concourse.bass as bass
from concourse import mybir

F32 = mybir.dt.float32
I32 = mybir.dt.int32
U32 = mybir.dt.uint32
ALU = mybir.AluOpType
ACT = mybir.ActivationFunctionType
AX_X = mybir.AxisListType.X

P = 128
D = 2048
KD = D // P
SEQ, NB_P = 512, 4
DECB, DECT = 8, 4
NS = DECB * DECT
NTOK = SEQ + NS
BLOCKS = 5
ROWS = [P] * NB_P + [NS]
H, DH = 8, 128
AW = H * DH
G = 8
PAST = 2048
EPS = 1e-6
SCALE = DH ** -0.5
WINDOWS = ((128, 1), (512, 4), (2048, 16))
NEG = -1.0e30
NKEY = 128
PH = 8
TOPK = 16
SLOTS = PH * TOPK
NC = 512
ADA_T = 6 * D // NC
IN_T = (3 * AW + 2 * AW) // NC
OUT_T = D // NC
CH = 7
FAR = 3
NK = CH * P
NKS = NK + NS
GRP = 8
RING = 4

W0 = 0
HT0 = W0 + 2 * KD * NC
MT0 = HT0 + KD * NTOK
Q0 = MT0 + KD * NTOK
K0 = Q0 + BLOCKS * AW
V0 = K0 + BLOCKS * AW
C0 = V0 + BLOCKS * AW
WORDS = C0 + 3900
QUAD = 32
EV = BLOCKS + 1
EV_OF = [1, 3, 4, 5, 2]
BANK_OF = [0, 1, 2, 3, 6]


def tickets():
    order = [("c",), ("ws", 0), ("ws", 1), ("wd",), ("sk",)]
    order += [("h", b, g) for b in range(BLOCKS) for g in range(4)]
    for b in range(BLOCKS):
        order += [("m", b, 0), ("m", b, 1)]
    for b in range(BLOCKS):
        order += [("mt", b, 0), ("mt", b, 1)]
    order += [("q", 0), ("k", 0)]
    for h in range(H):
        if h + 1 < H:
            order += [("q", h + 1), ("k", h + 1)]
        order += [("p", h, j) for j in range(NB_P)]
    order += [("qs",), ("ks",)]
    order += [("kt", 0, h, i) for h in range(2) for i in range(2)]
    for b in range(DECB):
        order += [("kt", b, h, i) for h in range(2, H) for i in range(2)]
        if b + 1 < DECB:
            order += [("kt", b + 1, h, i) for h in range(2) for i in range(2)]
        order += [("pt", b, 0), ("pt", b, 1), ("ot", b)]
    order += [("h2", b, g) for b in range(BLOCKS) for g in range(4)]
    return {key: n for n, key in enumerate(order)}


def trunk_step(nc, x_prompt, x_sample, cache_k, cache_v, c_prompt, c_sample, w_ada, b_ada, g_norm1, w_in,
               ln_v_g, ln_v_b, w_spatial, b_spatial, w_out, g_norm2, w_query, sub_keys, expert_u, expert_v,
               g_final, y_prompt, y_sample, k_win, v_win, k_new, v_new, sgu_v):
    T = tickets()
    ctx = ExitStack()
    with ctx:
        arena = ctx.enter_context(nc.sbuf_tensor("arena", [P, WORDS], F32))
        ps = ctx.enter_context(nc.psum_tensor("ps", [P, 8, NC], F32))
        mod_dram = nc.dram_tensor("modulation", (1 + DECB, 6 * D), F32, kind="Internal").ap()

        def sem(name):
            return ctx.enter_context(nc.semaphore(name))

        def at(offset, *shape, rows=P):
            n = math.prod(shape)
            v = arena[0:rows, offset:offset + n]
            if len(shape) == 2:
                v = v.rearrange("p (a b) -> p a b", b=shape[1])
            if len(shape) == 3:
                v = v.rearrange("p (a b c) -> p a b c", b=shape[1], c=shape[2])
            return v

        cursor = [C0]

        def const(*shape, rows=P):
            v = at(cursor[0], *shape, rows=rows)
            cursor[0] += math.prod(shape)
            assert cursor[0] <= WORDS
            return v

        xp, xs = x_prompt.rearrange("a s d -> (a s) d"), x_sample.rearrange("b t d -> (b t) d")
        yp, ys = y_prompt.rearrange("a s d -> (a s) d"), y_sample.rearrange("b t d -> (b t) d")
        kwp, vwp = (w.rearrange("l b s h c -> (l b s) (h c)") for w in (k_win, v_win))
        knp, vnp = (w.rearrange("l b s h c -> (l b s) (h c)") for w in (k_new, v_new))
        sgp = sgu_v.rearrange("l b t d -> (l b t) d")
        x_of = [xp[b * P:(b + 1) * P, :] for b in range(NB_P)] + [xs]
        y_of = [yp[b * P:(b + 1) * P, :] for b in range(NB_P)] + [ys]
        u_rows = expert_u.rearrange("l e d -> (l e) d")
        v_rows = expert_v.rearrange("l e d -> (l e) d")

        ident = const(P)
        c_t = const(KD, QUAD)
        partial = const(NC)
        sel = const(QUAD)
        delta = const(SEQ)
        count_ln = const(SEQ)
        bias_s = const(NKS)
        bias_new = const(DECB, NS)
        slope_s = const(1)
        stat = const(64)
        bs_p = const(G)
        bs_s = const(G, rows=NS)
        sub_t = const(2, NKEY)
        iota16 = const(TOPK)
        iota_i = const(TOPK).bitcast(I32)
        idx_stage = const(2, GRP).bitcast(I32)
        act_sum = const(2, GRP)
        act_gelu = const(2, GRP)
        coef = const(2, GRP)

        mod = at(HT0, 6 * D, rows=1 + DECB)
        c_in = at(K0 + NB_P * D, D, rows=1 + DECB)
        g1_rows, g2_rows = (at(HT0 + 6 * D + D * i, D, rows=1 + DECB) for i in range(2))
        assert HT0 + 8 * D <= Q0
        w_slot = [at(W0 + s * KD * NC, KD, NC) for s in range(2)]
        tmp_i = [at(K0 + 2 * D + 1024 * i, NKS) for i in range(4)]

        scale1_p, shift1_p, scale1_s, shift1_s = (at(MT0 + D * i, D) for i in range(4))
        x_buf = h_buf = [at(K0 + D * b, D) for b in range(BLOCKS)]
        h_t = at(HT0, KD, NTOK)

        mix_t = at(MT0, KD, NTOK)
        q_all, k_all, v_all = (at(o, BLOCKS, AW) for o in (Q0, K0, V0))
        u_all, g_all = k_all, v_all
        ln_g, ln_b = at(Q0, AW), at(Q0 + AW, AW)
        ws_in, ws_t = at(Q0 + 2 * AW, G, P), at(Q0 + 3 * AW, G, P)
        wd_in, wd_t = at(Q0 + 4 * AW, G, NS, rows=NS), at(Q0 + 4 * AW + G * NS, G, NS, rows=NS)

        o = HT0
        head_bias = at(o, SEQ); o += SEQ
        q_t = [at(o + SEQ * i, SEQ) for i in range(2)]; o += 2 * SEQ
        k_t = [at(o + SEQ * i, SEQ) for i in range(2)]; o += 2 * SEQ
        prob = []
        for qi in range(NB_P):
            prob.append(at(o, (qi + 1) * P)); o += (qi + 1) * P
        prob_t = at(o, NB_P, SEQ); o += NB_P * SEQ
        assert o <= MT0

        KVW = CH * AW
        kv_k = [at(0, CH, AW), at(2 * KVW, CH, AW)]
        kv_v = [at(KVW, CH, AW), at(Q0, CH, AW)]
        key_t = [at(Q0 + KVW + NK * i, NK) for i in range(2)]
        assert Q0 + KVW + 2 * NK <= K0 + NB_P * AW
        o = 3 * KVW
        prob_s = at(o, NKS); o += NKS
        prob_st = at(o, CH + 1, P); o += (CH + 1) * P
        att_s = at(o, 2, P); o += 2 * P
        q_mask = [at(o + 256 * i, H, NS) for i in range(2)]; o += 512
        q_st = at(o, H, NS); o += 256
        k_st = at(o, H, NS); o += 256
        assert o <= MT0

        x1 = at(Q0, BLOCKS, D)
        gate1_p, gate1_s = at(HT0, D), at(HT0 + D, D)
        scale2_p, shift2_p = at(HT0 + 2 * D, D), at(HT0 + 3 * D, D)
        scale2_s, shift2_s = at(V0, D), at(V0 + D, D)
        gated = [at(V0 + 2 * D + 512 * i, NC) for i in range(2)]
        h2 = [at(W0 + KD * NC + D * b, D) for b in range(NB_P)] + [at(HT0, D)]
        h2_t = at(MT0, KD, NTOK)

        wq_slot = [at(W0 + s * KD * 256, KD, 256) for s in range(2)]
        o = HT0 + D
        qry_t = [at(o + NTOK * i, NTOK) for i in range(2)]; o += 2 * NTOK
        top_s = at(o, BLOCKS, 2, TOPK); o += BLOCKS * 2 * TOPK
        top_i = at(o, BLOCKS, 2, TOPK).bitcast(U32); o += BLOCKS * 2 * TOPK
        top_f, gate_sum = at(o, BLOCKS, 2, TOPK), at(o, NB_P * PH); o += BLOCKS * 2 * TOPK
        cut = at(o, BLOCKS, NKEY); o += BLOCKS * NKEY
        cand = at(o, BLOCKS, TOPK * TOPK)
        pick = [at(o + i * BLOCKS * TOPK * TOPK, BLOCKS, TOPK * TOPK) for i in range(2)]; o += 2 * BLOCKS * TOPK * TOPK
        cand_cut = pick[1]
        best_s = at(o, BLOCKS, TOPK); o += BLOCKS * TOPK
        best_j = at(o, BLOCKS, TOPK).bitcast(U32); o += BLOCKS * TOPK
        best_ab = [at(o + i * BLOCKS * TOPK, BLOCKS, TOPK).bitcast(U32) for i in range(2)]; o += 2 * BLOCKS * TOPK
        best_abf = [at(o + i * BLOCKS * TOPK, BLOCKS, TOPK) for i in range(2)]; o += 2 * BLOCKS * TOPK
        key_f = [at(o + i * BLOCKS * TOPK, BLOCKS, TOPK) for i in range(2)]; o += 2 * BLOCKS * TOPK
        assert o <= MT0
        idx_all = at(V0, BLOCKS, SLOTS).bitcast(I32)
        gate_all = at(V0 + BLOCKS * SLOTS, BLOCKS, SLOTS)
        sub_in = at(Q0 + 4 * AW + 2 * G * NS, 2, NKEY)

        u_slot = [at(W0 + D * i, D) for i in range(RING)]
        v_slot = [at(MT0 + D * i, D) for i in range(RING)]
        gate2_p, gate2_s, g_fin = (at(HT0 + D + D * i, D) for i in range(3))
        diag = [at(V0 + 3 * AW + P * i, P) for i in range(GRP)]
        idx_rep = at(V0 + 2 * BLOCKS * SLOTS + NS, NS).bitcast(I32)
        gate_rep = at(V0 + 2 * BLOCKS * SLOTS + 2 * NS, NS)
        out_buf = at(MT0 + RING * D, 16)

        in_c, in_rows, in_ws, in_wd, in_misc, in_bada = (sem(n) for n in ("in_c", "in_rows", "in_ws", "in_wd", "in_misc", "in_bada"))
        w_loaded = [sem(f"w_loaded{s}") for s in range(2)]
        pool_const = sem("pool_const")
        silu_done = sem("silu_done")
        ada_full, ada_free = sem("ada_full"), sem("ada_free")
        mod_ready, mod_stored = sem("mod_ready"), sem("mod_stored")
        mod_loaded = sem("mod_loaded")
        turn_full = [sem(f"turn_full{i}") for i in range(3)]
        turn_free = [sem(f"turn_free{i}") for i in range(3)]
        x_loaded = [sem(f"x_loaded{i}") for i in range(BLOCKS)]
        tables_done = sem("tables_done")
        norm_sq, norm_ms, norm_rt, norm_h = sem("norm_sq"), sem("norm_ms"), sem("norm_rt"), sem("norm_h")
        bank_full, bank_free = sem("bank_full"), sem("bank_free")
        ln_var, ln_rt, ln_done = sem("ln_var"), sem("ln_rt"), sem("ln_done")
        tri_done = sem("tri_done")
        sgu_stored = sem("sgu_stored")
        kv_stored = sem("kv_stored")
        dve = sem("dve_step")
        s_full, s_free = sem("s_full"), sem("s_free")
        biased, normed, exped = sem("biased"), sem("normed"), sem("exped")
        o_full, o_free = sem("o_full"), sem("o_free")
        kvk_loaded = [sem(f"kvk_loaded{i}") for i in range(2)]
        kvv_loaded = [sem(f"kvv_loaded{i}") for i in range(2)]
        ss_full, ss_free = sem("ss_full"), sem("ss_free")
        s_biased, s_exped, s_normed = sem("s_biased"), sem("s_exped"), sem("s_normed")
        os_full, os_free = sem("os_full"), sem("os_free")
        q_masked = sem("q_masked")
        new_turned = sem("new_turned")
        x1_loaded, mod2_loaded = sem("x1_loaded"), sem("mod2_loaded")
        x1_done = sem("x1_done")
        qry_full, qry_free = sem("qry_full"), sem("qry_free")
        sc_full, sc_free = sem("sc_full"), sem("sc_free")
        picked, gate_exp = sem("picked"), sem("gate_exp")
        gates_done, rep_loaded, peer_tables = sem("gates_done"), sem("rep_loaded"), sem("peer_tables")
        u_loaded = [sem(f"u_loaded{i}") for i in range(RING)]
        v_loaded = [sem(f"v_loaded{i}") for i in range(RING)]
        u_done, v_done = sem("u_done"), sem("v_done")
        pool_go = sem("pool_go")
        idx_copied = sem("idx_copied")
        gelu_done, coef_done, diag_done = sem("gelu_done"), sem("coef_done"), sem("diag_done")
        zeroed = sem("zeroed")
        fin_x, fin_sq, fin_ms, fin_rt, fin_y, y_stored = (sem(n) for n in ("fin_x", "fin_sq", "fin_ms", "fin_rt", "fin_y", "y_stored"))

        def turn(key):
            return 5 + T[key] % 3, T[key] // 3

        def wait_turn_free(eng, key):
            bank, n = turn(key)
            if n:
                eng.wait_ge(turn_free[bank - 5], n)
            return bank

        def turned(ins, key):
            ins.then_inc(turn_full[turn(key)[0] - 5], 1)

        def wait_turn_full(eng, key):
            bank, n = turn(key)
            eng.wait_ge(turn_full[bank - 5], n + 1)
            return bank

        def turn_read(ins, key):
            ins.then_inc(turn_free[turn(key)[0] - 5], 1)

        def wait_turn_read(eng, key):
            bank, n = turn(key)
            eng.wait_ge(turn_free[bank - 5], n + 1)

        def tok(b):
            return slice(b * P, b * P + ROWS[b])

        IN_ORDER = [8, 9, 6, 7, 0, 1, 2, 3, 4, 5]
        A_USES, IN_USES = ADA_T // 2, IN_T // 2
        T_IN, T_OUT, T_Q = ADA_T, ADA_T + IN_T, ADA_T + IN_T + OUT_T
        w_ada_v = w_ada.rearrange("l (k p) n -> p (l k) n", p=P)
        w_in_v = w_in.rearrange("l (k p) n -> p (l k) n", p=P)
        w_out_v = w_out.rearrange("l (k p) n -> p (l k) n", p=P)
        w_query_v = w_query.rearrange("l (k p) n -> p (l k) n", p=P)

        block = ctx.enter_context(nc.Block())

        @block.sync
        def _(sp):
            sp.dma_start(c_in[0:1, :], c_prompt).then_inc(in_c, 16)
            sp.dma_start(c_in[1:1 + DECB, :], c_sample).then_inc(in_c, 16)
            for b in range(2):
                sp.dma_start(x_buf[b], x_of[b]).then_inc(x_loaded[b], 16)

            def tile_used(t):
                if t < T_IN:
                    sp.wait_ge(ada_full, 2 * t + 1)
                elif t < T_Q:
                    sp.wait_ge(bank_full, (t - T_IN + 1) * EV)
                else:
                    sp.wait_ge(qry_full, 4 * (t - T_Q + 1))

            def load_w(t, dst, src):
                if t >= 2:
                    tile_used(t - 2)
                sp.dma_start(dst, src).then_inc(w_loaded[t % 2], 16)

            for n in range(ADA_T):
                load_w(n, w_slot[n % 2], w_ada_v[:, :, n * NC:(n + 1) * NC])
            for i, n in enumerate(IN_ORDER):
                load_w(T_IN + i, w_slot[i % 2], w_in_v[:, :, n * NC:(n + 1) * NC])

            def load_cache(cache, b, dst, s):
                rows = cache.rearrange("l b s h c -> (l b) s (h c)")[b]
                for c in range(FAR):
                    far = bass.AP(rows.tensor, rows.offset + 512 * c * AW, [[16 * AW, 32], [AW, 4], [1, AW]])
                    sp.dma_start(dst[:, c, :], far).then_inc(s, 16)
                near = rows[PAST - 512:PAST, :].rearrange("(c p) n -> p c n", p=P)
                sp.dma_start(dst[:, FAR:CH, :], near).then_inc(s, 16)

            tile_used(T_OUT - 1)
            for b in range(DECB):
                if b == 1:
                    sp.wait_ge(o_full, H)
                    sp.wait_ge(o_free, H)
                    sp.wait_ge(turn_free[turn(("qs",))[0] - 5], turn(("qs",))[1] + 1)
                    sp.wait_ge(kv_stored, 16 * 2 * BLOCKS)
                if b >= 2:
                    sp.wait_ge(os_full, b - 1)
                load_cache(cache_k, b, kv_k[b % 2], kvk_loaded[b % 2])
                load_cache(cache_v, b, kv_v[b % 2], kvv_loaded[b % 2])
            sp.wait_ge(os_full, DECB)
            for n in range(OUT_T):
                load_w(T_OUT + n, w_slot[n % 2], w_out_v[:, :, n * NC:(n + 1) * NC])
            for h in range(PH):
                if h == 0:
                    tile_used(T_Q - 1)
                load_w(T_Q + h, wq_slot[h % 2], w_query_v[:, :, h * 256:(h + 1) * 256])

        @block.gpsimd
        def _(pool):
            steps = [0]

            def step(ins):
                steps[0] += 1
                ins.then_inc(pool_const, 1)
                pool.wait_ge(pool_const, steps[0])

            step(nc.gpsimd.memset(ident, 0.0))
            step(nc.gpsimd.affine_select(out=ident, in_=ident, compare_op=ALU.not_equal, fill=1.0, base=0,
                                         pattern=[[-1, P]], channel_multiplier=1))
            pool.dma_start(mod, b_ada[0].partition_broadcast(1 + DECB)).then_inc(in_bada, 16)
            pool.dma_start(g1_rows, g_norm1[0].partition_broadcast(1 + DECB)).then_inc(in_rows, 16)
            pool.dma_start(g2_rows, g_norm2[0].partition_broadcast(1 + DECB)).then_inc(in_rows, 16)
            step(nc.gpsimd.iota(tmp_i[0][:, 0:SEQ].bitcast(I32), pattern=[[-1, SEQ]], base=SEQ - P, channel_multiplier=1))
            step(nc.gpsimd.iota(tmp_i[1][:, 0:FAR * P].rearrange("p (m r) -> p m r", r=4).bitcast(I32),
                                pattern=[[-16, FAR * 32], [-1, 4]], base=PAST, channel_multiplier=0))
            step(nc.gpsimd.iota(tmp_i[1][:, FAR * P:NK].bitcast(I32), pattern=[[-1, 512]], base=512, channel_multiplier=0))
            step(nc.gpsimd.iota(tmp_i[1][:, NK:NKS].rearrange("p (b t) -> p b t", t=DECT).bitcast(I32),
                                pattern=[[0, DECB], [-1, DECT]], base=0, channel_multiplier=0))
            step(nc.gpsimd.memset(c_t, 0.0))
            step(nc.gpsimd.iota(iota_i, pattern=[[1, TOPK]], base=0, channel_multiplier=0))
            step(nc.gpsimd.iota(slope_s.bitcast(I32), pattern=[[0, 1]], base=0, channel_multiplier=1))
            step(nc.gpsimd.memset(bias_new, 0.0))
            v = bias_new.rearrange("p b (k t) -> p b k t", t=DECT)
            step(nc.gpsimd.affine_select(out=v, in_=v, compare_op=ALU.is_equal, fill=NEG, base=0,
                                         pattern=[[1, DECB], [-1, DECB], [0, DECT]], channel_multiplier=0))
            pool.dma_start(ws_in, w_spatial[0].rearrange("g t s -> t g s")).then_inc(in_ws, 16)
            pool.dma_start(ln_g, ln_v_g[0].partition_broadcast(P)).then_inc(in_misc, 16)
            pool.dma_start(ln_b, ln_v_b[0].partition_broadcast(P)).then_inc(in_misc, 16)
            pool.dma_start(bs_p, b_spatial[0].rearrange("g t -> t g"), allow_slow_non_contiguous=True).then_inc(in_misc, 16)
            step(nc.gpsimd.memset(wd_in, 0.0))
            for b in range(DECB):
                r = slice(DECT * b, DECT * b + DECT)
                pool.dma_start(wd_in[r, :, r], w_spatial[0, :, 0:DECT, 0:DECT].rearrange("g t s -> t g s")).then_inc(in_wd, 16)
                pool.dma_start(bs_s[r, :], b_spatial[0, :, 0:DECT].rearrange("g t -> t g"), allow_slow_non_contiguous=True).then_inc(in_misc, 16)
            pool.dma_start(sub_in, sub_keys[0].rearrange("j n c -> n j c")).then_inc(in_misc, 16)
            pool.wait_ge(in_ws, 16)
            nc.gpsimd.affine_select(out=ws_in, in_=ws_in, compare_op=ALU.is_ge, fill=0.0, base=0,
                                    pattern=[[0, G], [-1, P]], channel_multiplier=1).then_inc(tri_done, 1)
            pool.wait_ge(in_wd, 16 * DECB)
            nc.gpsimd.affine_select(out=wd_in, in_=wd_in, compare_op=ALU.is_ge, fill=0.0, base=0,
                                    pattern=[[0, G], [-1, NS]], channel_multiplier=1).then_inc(tri_done, 1)

            pool.wait_ge(tables_done, 1)
            wait_turn_full(pool, ("c",))
            for b in range(2, BLOCKS):
                pool.dma_start(x_buf[b][0:ROWS[b], :], x_of[b]).then_inc(x_loaded[b], 16)

            pool.wait_ge(mod_ready, 2)
            pool.dma_start(mod_dram, mod).then_inc(mod_stored, 16)
            pool.wait_ge(mod_stored, 16)

            def load_mod(part_of, dst_p, dst_s, s):
                cols = slice(part_of * D, (part_of + 1) * D)
                pool.dma_start(dst_p, mod_dram[0, cols].partition_broadcast(P)).then_inc(s, 16)
                row = mod_dram[1, cols]
                pool.dma_start(dst_s[0:NS, :], bass.AP(row.tensor, row.offset, [[6 * D, DECB], [0, DECT], [1, D]])).then_inc(s, 16)

            load_mod(0, shift1_p, shift1_s, mod_loaded)
            load_mod(1, scale1_p, scale1_s, mod_loaded)

            pool.wait_ge(ln_done, BLOCKS)
            pool.dma_start(sgp, g_all[0:NS, NB_P, :]).then_inc(sgu_stored, 16)
            for i, (src, win, new) in enumerate(((k_all, kwp, knp), (v_all, vwp, vnp))):
                for b in range(BLOCKS):
                    pool.wait_ge(bank_free, EV + (7 + 2 * i) * EV + EV_OF[b] + 1)
                    dst = win[b * P:(b + 1) * P, :] if b < NB_P else new
                    pool.dma_start(dst, src[0:ROWS[b], b, :]).then_inc(kv_stored, 16)

            wait_turn_read(pool, ("ot", DECB - 1))
            pool.wait_ge(kv_stored, 16 * 2 * BLOCKS)
            for b in range(BLOCKS):
                pool.dma_start(x1[0:ROWS[b], b, :], x_of[b]).then_inc(x1_loaded, 16)
            load_mod(2, gate1_p, gate1_s, mod2_loaded)
            load_mod(3, shift2_p, shift2_s, mod2_loaded)
            load_mod(4, scale2_p, scale2_s, mod2_loaded)

            pool.wait_ge(gates_done, 2)
            load_mod(5, gate2_p, gate2_s, peer_tables)
            pool.dma_start(g_fin, g_final.partition_broadcast(P)).then_inc(peer_tables, 16)
            for q in range(4):
                r = slice(NS * q, NS * q + NS)
                pool.dma_start(idx_rep[r, :], idx_all[0:NS, NB_P, r]).then_inc(rep_loaded, 16)
                pool.dma_start(gate_rep[r, :], gate_all[0:NS, NB_P, r]).then_inc(rep_loaded, 16)
                if q:
                    pool.dma_start(h2[NB_P][r, :], h2[NB_P][0:NS, :]).then_inc(rep_loaded, 16)

            def gather_groups(src, first, i):
                for par in range(2):
                    n = first + par
                    pool.wait_ge(v_done, n * GRP + 1)
                    pool.sem_inc(pool_go, 1)
                    nc.gpsimd.tensor_copy(idx_stage[:, par, :], src[:, bass.ds(i * 2 * GRP + par * GRP, GRP)]).then_inc(idx_copied, 1)
                    pool.wait_ge(idx_copied, n + 1)
                    for table, slots, loaded, done, ahead in (
                            (u_rows, u_slot, u_loaded, u_done, RING), (v_rows, v_slot, v_loaded, v_done, GRP)):
                        for k in range(GRP):
                            pool.wait_ge(done, n * GRP + k + 1 + ahead - RING)
                            pool.sem_inc(pool_go, 1)
                            nc.gpsimd.indirect_dma_start(
                                out=slots[k % RING], out_offset=None, in_=table,
                                in_offset=bass.IndirectOffsetOnAxis(ap=idx_stage[:, par, k:k + 1], axis=0),
                            ).then_inc(loaded[k % RING], 16)

            pool.wait_ge(rep_loaded, 16 * 11)
            pairs = SLOTS // GRP // 2
            for b in range(NB_P):
                with pool.Fori(0, pairs) as i:
                    gather_groups(idx_all[:, b, :], i * 2 + b * 2 * pairs, i)
            with pool.Fori(0, pairs // 4) as i:
                gather_groups(idx_rep, i * 2 + NB_P * 2 * pairs, i)

        @block.scalar
        def _(act):
            act.wait_ge(in_c, 32)
            nc.scalar.activation(c_in, c_in, ACT.Silu).then_inc(silu_done, 1)

            def read_turn(key, dst, shape, rows=P):
                bank = wait_turn_full(act, key)
                src = ps[0:rows, bank, 0:math.prod(shape)]
                if len(shape) == 2:
                    src = src.rearrange("p (a b) -> p a b", b=shape[1])
                turn_read(nc.scalar.copy(dst, src), key)

            act.wait_ge(pool_const, 11)
            read_turn(("c",), c_t[:, :, 0:1 + DECB], (KD, 1 + DECB))
            for i in range(2):
                read_turn(("ws", i), ws_t[:, 4 * i:4 * i + 4, :], (4, P))
            read_turn(("wd",), wd_t, (G, NS), rows=NS)
            read_turn(("sk",), sub_t, (2, NKEY))

            def norm_rows(u, x, h, b, wait):
                wait()
                nc.scalar.activation(h[0:ROWS[b], :], x[0:ROWS[b], :], ACT.Square,
                                     accum_out=stat[0:ROWS[b], u:u + 1]).then_inc(norm_sq, 1)
                act.wait_ge(norm_ms, u + 1)
                nc.scalar.activation(stat[0:ROWS[b], u:u + 1], stat[0:ROWS[b], u:u + 1], ACT.Sqrt).then_inc(norm_rt, 1)

            for b in range(BLOCKS):
                act.wait_ge(norm_ms, b + 1)
                nc.scalar.activation(stat[0:ROWS[b], b:b + 1], stat[0:ROWS[b], b:b + 1], ACT.Sqrt).then_inc(norm_rt, 1)
            for b in range(BLOCKS):
                for g in range(4):
                    read_turn(("h", b, g), h_t[:, 4 * g:4 * g + 4, tok(b)], (4, ROWS[b]))

            def read_tile(i, dst, func):
                act.wait_ge(bank_full, i * EV + 1)
                nc.scalar.copy(partial, ps[:, 4, :]).then_inc(bank_free, 1)
                for b in (0, NB_P, 1, 2, 3):
                    act.wait_ge(bank_full, i * EV + EV_OF[b] + 1)
                    nc.scalar.activation(dst[0:ROWS[b], b, (i % 2) * NC:(i % 2 + 1) * NC], ps[0:ROWS[b], BANK_OF[b], :],
                                         func).then_inc(bank_free, 1)

            for i in range(2):
                read_tile(i, g_all, ACT.Gelu)
            for b in range(BLOCKS):
                act.wait_ge(ln_var, b + 1)
                nc.scalar.activation(stat[0:ROWS[b], 10 + b:11 + b], stat[0:ROWS[b], 10 + b:11 + b], ACT.Sqrt).then_inc(ln_rt, 1)
            for i in range(2, 4):
                read_tile(i, u_all, ACT.Gelu)
            for b in range(BLOCKS):
                for i in range(2):
                    read_turn(("mt", b, i), mix_t[:, H + 4 * i:H + 4 * i + 4, tok(b)], (4, ROWS[b]))
            for i in range(4, 10):
                if i == 8:
                    act.wait_ge(sgu_stored, 16)
                read_tile(i, (q_all, k_all, v_all)[i // 2 - 2], ACT.Copy)

            def turn_heads(h):
                if h >= 2:
                    act.wait_ge(s_full, NB_P * (h - 1))
                read_turn(("q", h), q_t[h % 2], (SEQ,))
                read_turn(("k", h), k_t[h % 2], (SEQ,))

            turn_heads(0)
            for h in range(H):
                if h + 1 < H:
                    turn_heads(h + 1)
                act.wait_ge(biased, h + 1)
                for qi in range(NB_P):
                    nc.scalar.activation(prob[qi], prob[qi], ACT.Exp, bias=stat[:, 32 + qi:33 + qi],
                                         accum_out=stat[:, 36 + qi:37 + qi]).then_inc(exped, 1)
                for j in range(NB_P):
                    if j == 0 and h:
                        act.wait_ge(o_full, h)
                    bank = wait_turn_full(act, ("p", h, j))
                    turn_read(nc.scalar.copy(prob_t[:, j, j * P:SEQ], ps[:, bank, 0:SEQ - j * P]), ("p", h, j))
                act.wait_ge(o_full, h + 1)
                nc.scalar.copy(mix_t[:, h, 0:SEQ], ps[:, 4, :]).then_inc(o_free, 1)

            act.wait_ge(kv_stored, 16 * 2 * BLOCKS)
            read_turn(("qs",), q_st, (H, NS))
            read_turn(("ks",), k_st, (H, NS))

            def turn_key(b, h, i):
                read_turn(("kt", b, h, i), key_t[h % 2][:, 512 * i:min(512 * i + 512, NK)], (min(512, NK - 512 * i),))

            for b in range(DECB):
                for h in range(2 if b else 0, H):
                    for i in range(2):
                        if i == 0 and b * H + h >= 2:
                            act.wait_ge(ss_full, b * H + h - 1)
                        if (h + i) % 2 == 0:
                            turn_key(b, h, i)
                act.wait_ge(s_biased, b + 1)
                nc.scalar.activation(prob_s, prob_s, ACT.Exp, bias=stat[:, 40:41],
                                     accum_out=stat[:, 41:42]).then_inc(s_exped, 1)
                if b + 1 < DECB:
                    for h in range(2):
                        for i in range(2):
                            if i == 0:
                                act.wait_ge(ss_full, b * H + H - 1 + h)
                            if (h + i) % 2 == 0:
                                turn_key(b + 1, h, i)
                bank = wait_turn_full(act, ("pt", b, 1))
                nc.scalar.copy(prob_st[0:NS, CH, :], ps[0:NS, bank, (CH - 4) * P:(CH - 3) * P]).then_inc(new_turned, 1)
                read_turn(("pt", b, 1), prob_st[:, 4:CH, :], (CH - 4, P))
                act.wait_ge(os_full, b + 1)
                nc.scalar.copy(att_s, ps[:, 3, 0:2 * P].rearrange("p (g n) -> p g n", n=P)).then_inc(os_free, 1)
                key = ("ot", b)
                bank = wait_turn_full(act, key)
                src = ps[:, bank, 0:2 * P]
                m = mix_t[:, 0:H, SEQ + DECT * b:SEQ + DECT * b + DECT]
                turn_read(nc.scalar.copy(m.rearrange("p (g j) t -> p g j t", j=4),
                                         bass.AP(src.tensor, src.offset, [src.ap[0], [P + 4 * DECT, 2], [QUAD + DECT, 4], [1, DECT]])), key)

            for b in range(BLOCKS):
                def wait(b=b):
                    act.wait_ge(x1_done, BLOCKS * OUT_T)
                norm_rows(BLOCKS + b, x1[:, b, :], h2[b], b, wait)
                if b:
                    for g in range(4):
                        read_turn(("h2", b - 1, g), h2_t[:, 4 * g:4 * g + 4, tok(b - 1)], (4, ROWS[b - 1]))
            for g in range(4):
                read_turn(("h2", NB_P, g), h2_t[:, 4 * g:4 * g + 4, tok(NB_P)], (4, NS))

            with act.Fori(0, PH) as h:
                act.wait_ge(qry_full, h * 4 + 1)
                nc.scalar.copy(partial[:, 0:2 * P], ps[:, 1, 0:2 * P]).then_inc(qry_free, 1)
                act.wait_ge(qry_full, h * 4 + 2)
                nc.scalar.copy(qry_t[0][:, 0:SEQ], ps[:, 0, :]).then_inc(qry_free, 1)
                act.wait_ge(qry_full, h * 4 + 3)
                for j in range(2):
                    nc.scalar.copy(qry_t[j][:, SEQ:NTOK], ps[:, 3, j * NS:(j + 1) * NS]).then_inc(qry_free, 1)
                act.wait_ge(qry_full, h * 4 + 4)
                nc.scalar.copy(qry_t[1][:, 0:SEQ], ps[:, 2, :]).then_inc(qry_free, 1)

            act.wait_ge(gates_done, 1)
            g_flat = gate_all.rearrange("p b s -> p (b s)")
            nc.scalar.activation(g_flat[:, 0:NB_P * SLOTS], g_flat[:, 0:NB_P * SLOTS], ACT.Exp).then_inc(gate_exp, 1)
            nc.scalar.activation(g_flat[0:NS, NB_P * SLOTS:], g_flat[0:NS, NB_P * SLOTS:], ACT.Exp).then_inc(gate_exp, 1)

            def groups(n0):
                for par in range(2):
                    n = n0 + par
                    act.wait_ge(u_done, n * GRP + GRP + RING)
                    nc.scalar.activation(act_gelu[:, par, :], act_sum[:, par, :], ACT.Gelu).then_inc(gelu_done, 1)
                    act.wait_ge(coef_done, n + 1)
                    for k in range(GRP):
                        act.wait_ge(v_done, n * GRP + k + 1)
                        if is_sample[0]:
                            nc.scalar.activation(diag[k][:, 0:NS], sel, ACT.Copy, scale=coef[:, par, k:k + 1]).then_inc(diag_done, 1)
                        else:
                            nc.scalar.activation(diag[k], ident, ACT.Copy, scale=coef[:, par, k:k + 1]).then_inc(diag_done, 1)

            def finish(b):
                r = ROWS[b]
                act.wait_ge(fin_x, b + 1)
                bank = 4 * (b % 2)
                nc.scalar.activation(ps[0:r, bank:bank + 4, :].rearrange("p a n -> p (a n)"), x1[0:r, b, :], ACT.Square,
                                     accum_out=stat[0:r, 48 + b:49 + b]).then_inc(fin_sq, 1)
                act.wait_ge(fin_ms, b + 1)
                nc.scalar.activation(stat[0:r, 48 + b:49 + b], stat[0:r, 48 + b:49 + b], ACT.Sqrt).then_inc(fin_rt, 1)
                act.wait_ge(fin_y, b + 1)
                act.dma_start(y_of[b], x1[0:r, b, :]).then_inc(y_stored, 16)

            is_sample = [False]
            pairs = SLOTS // GRP // 2
            for b in range(BLOCKS):
                is_sample[0] = b == NB_P
                base = b * 2 * pairs
                groups(base)
                if b:
                    finish(b - 1)
                with act.Fori(1, pairs if b < NB_P else pairs // 4) as i:
                    groups(i * 2 + base)
            finish(NB_P)
            act.wait_ge(y_stored, 16 * BLOCKS)
            act.wait_ge(sgu_stored, 16)
            act.wait_ge(kv_stored, 16 * 2 * BLOCKS)

        @block.vector
        def _(dv):
            chain = [0]
            V = nc.vector

            def link(ins):
                chain[0] += 1
                ins.then_inc(dve, 1)
                dv.wait_ge(dve, chain[0])

            dv.sem_inc(u_done, RING)
            dv.wait_ge(pool_const, 11)

            def branch_counts(di, df, c, t, ti, n, rows):
                di, df, c, t, ti = di[0:rows, 0:n], df[0:rows, 0:n], c[0:rows, 0:n], t[0:rows, 0:n], ti[0:rows, 0:n]
                link(V.tensor_scalar(c, df, float(WINDOWS[0][0]), None, ALU.is_le))
                for window, dil in WINDOWS[1:]:
                    link(V.tensor_scalar(ti.bitcast(I32), di.bitcast(I32), dil - 1, None, ALU.bitwise_and))
                    link(V.tensor_scalar(t, ti.bitcast(I32), 0.0, None, ALU.is_equal))
                    link(V.scalar_tensor_tensor(out=t, in0=df, scalar=float(window), in1=t, op0=ALU.is_le, op1=ALU.mult))
                    link(V.tensor_tensor(c, c, t, ALU.add))
                link(V.scalar_tensor_tensor(out=c, in0=df, scalar=0.0, in1=c, op0=ALU.is_ge, op1=ALU.mult))
                link(V.tensor_scalar(t, c, 0.0, NEG, ALU.is_equal, ALU.mult))
                link(V.tensor_scalar(ti, c, 2.0, math.log(2.0), ALU.is_equal, ALU.mult))
                link(V.tensor_tensor(t, t, ti, ALU.add))
                link(V.tensor_scalar(ti, c, 3.0, math.log(3.0), ALU.is_equal, ALU.mult))
                link(V.tensor_tensor(c, t, ti, ALU.add))

            link(V.tensor_copy(delta, tmp_i[0][:, 0:SEQ].bitcast(I32)))
            branch_counts(tmp_i[0], delta, count_ln, tmp_i[2], tmp_i[3], SEQ, P)
            row, head = stat[:, 60:61], stat[:, 61:62]
            dist_s = tmp_i[0][:, 0:NKS]
            link(V.tensor_scalar(row.bitcast(I32), slope_s.bitcast(I32), DECT - 1, None, ALU.bitwise_and))
            link(V.tensor_scalar(slope_s.bitcast(I32), slope_s.bitcast(I32), QUAD - 1, None, ALU.bitwise_and))
            link(V.tensor_scalar(head.bitcast(I32), slope_s.bitcast(I32), 2, None, ALU.logical_shift_right))
            link(V.tensor_copy(stat[:, 62:63], row.bitcast(I32)))
            link(V.tensor_copy(stat[:, 63:64], head.bitcast(I32)))
            link(V.tensor_scalar(dist_s, tmp_i[1][:, 0:NKS].bitcast(I32), stat[:, 62:63], None, ALU.add))
            link(V.tensor_copy(tmp_i[1][:, 0:NKS].bitcast(I32), dist_s))
            link(V.tensor_copy(iota16, iota_i))
            link(V.tensor_scalar(slope_s.bitcast(I32), stat[:, 63:64], -float(1 << 23), float(126 << 23), ALU.mult, ALU.add))
            branch_counts(tmp_i[1], dist_s, bias_s, tmp_i[2], tmp_i[3], NKS, P)
            link(V.tensor_scalar(tmp_i[2][:, 0:NKS], dist_s, slope_s, -1.0, ALU.mult, ALU.mult))
            link(V.tensor_tensor(bias_s, bias_s, tmp_i[2][:, 0:NKS], ALU.add))
            link(V.tensor_tensor(bias_new, bias_new, bias_s[:, NK:NKS].unsqueeze(1).broadcast_to([P, DECB, NS]), ALU.add))
            for q in range(4):
                r = slice(NS * q, NS * q + NS)
                link(V.tensor_copy(sel[r, :], ident[r, r]))
            dv.sem_inc(tables_done, 1)

            dv.wait_ge(in_bada, 16)

            def ada_pairs(first, end):
                with dv.Fori(first, end) as i:
                    for s in range(2):
                        dv.wait_ge(ada_full, i * 4 + 2 * s + 1)
                        V.tensor_copy(partial, ps[:, s, :]).then_inc(ada_free, 1)
                        dv.wait_ge(ada_full, i * 4 + 2 * s + 2)
                        m = mod[:, bass.ds((i * 2 + s) * NC, NC)]
                        V.tensor_tensor(m, ps[0:1 + DECB, 2 + s, :], m, ALU.add).then_inc(ada_free, 1)

            ada_pairs(0, 4)
            for b in range(BLOCKS):
                r = ROWS[b]
                dv.wait_ge(x_loaded[b], 16)
                st, mv = stat[0:r, 16:40], stat[0:r, 44:46]
                for i in range(4):
                    link(V.bn_stats(out=st[:, 6 * i:6 * i + 6], in_=x_buf[b][0:r, i * NC:(i + 1) * NC]))
                link(V.bn_aggr(out=mv, in_=st))
                link(V.scalar_tensor_tensor(out=stat[0:r, b:b + 1], in0=mv[:, 0:1], scalar=mv[:, 0:1], in1=mv[:, 1:2],
                                            op0=ALU.mult, op1=ALU.add))
                V.tensor_scalar(stat[0:r, b:b + 1], stat[0:r, b:b + 1], EPS, None, ALU.add).then_inc(norm_ms, 1)
                dv.wait_ge(norm_rt, b + 1)
                link(V.reciprocal(stat[0:r, b:b + 1], stat[0:r, b:b + 1]))
            ada_pairs(4, ADA_T // 2)
            dv.wait_ge(ada_free, 4 + 2 * ADA_T)
            dv.wait_ge(in_rows, 32)
            for j, gain in ((1, g1_rows), (4, g2_rows)):
                m = mod[:, j * D:(j + 1) * D]
                V.scalar_tensor_tensor(out=m, in0=m, scalar=1.0, in1=gain, op0=ALU.add, op1=ALU.mult).then_inc(mod_ready, 1)

            def norm(u, x, h, b, scale, shift):
                r = ROWS[b]
                x, h, scale, shift = x[0:r, :], h[0:r, :], scale[0:r, :], shift[0:r, :]
                s = stat[0:r, u:u + 1]
                dv.wait_ge(norm_sq, b + 1)
                V.tensor_scalar(s, s, 1.0 / D, EPS, ALU.mult, ALU.add).then_inc(norm_ms, 1)
                dv.wait_ge(norm_rt, u + 1)
                link(V.reciprocal(s, s))
                link(V.scalar_tensor_tensor(out=h, in0=x, scalar=s, in1=scale, op0=ALU.mult, op1=ALU.mult))
                V.tensor_tensor(h, h, shift, ALU.add).then_inc(norm_h, 1)

            dv.wait_ge(mod_loaded, 64)
            for b in range(BLOCKS):
                r = ROWS[b]
                scale, shift = (scale1_p, shift1_p) if b < NB_P else (scale1_s, shift1_s)
                link(V.scalar_tensor_tensor(out=h_buf[b][0:r, :], in0=x_buf[b][0:r, :], scalar=stat[0:r, b:b + 1],
                                            in1=scale[0:r, :], op0=ALU.mult, op1=ALU.mult))
                V.tensor_tensor(h_buf[b][0:r, :], h_buf[b][0:r, :], shift[0:r, :], ALU.add).then_inc(norm_h, 1)

            dv.wait_ge(in_misc, 16 * (3 + DECB + 1))
            for b in range(BLOCKS):
                r = ROWS[b]
                g = g_all[0:r, b, :]
                st, mv, sd = stat[0:r, 20:32], stat[0:r, 44:46], stat[0:r, 10 + b:11 + b]
                dv.wait_ge(bank_free, EV + EV + EV_OF[b] + 1)
                for i in range(2):
                    link(V.bn_stats(out=st[:, 6 * i:6 * i + 6], in_=g[:, i * NC:(i + 1) * NC]))
                link(V.bn_aggr(out=mv, in_=st))
                V.tensor_scalar(sd, mv[:, 1:2], EPS, None, ALU.add).then_inc(ln_var, 1)
                dv.wait_ge(ln_rt, b + 1)
                link(V.reciprocal(sd, sd))
                link(V.tensor_scalar(g, g, mv[:, 0:1], sd, ALU.subtract, ALU.mult))
                link(V.tensor_tensor(g, g, ln_g[0:r, :], ALU.mult))
                V.tensor_tensor(g, g, ln_b[0:r, :], ALU.add).then_inc(ln_done, 1)
            dv.wait_ge(bank_free, EV + 4 * EV)
            for b in range(BLOCKS):
                r = ROWS[b]
                bs = bs_p if b < NB_P else bs_s
                for i in range(2):
                    bank = wait_turn_full(dv, ("m", b, i))
                    for g in range(4):
                        cols = slice((4 * i + g) * P, (4 * i + g + 1) * P)
                        ins = V.scalar_tensor_tensor(out=u_all[0:r, b, cols], in0=ps[0:r, bank, g * P:(g + 1) * P],
                                                     scalar=bs[0:r, 4 * i + g:4 * i + g + 1], in1=u_all[0:r, b, cols],
                                                     op0=ALU.add, op1=ALU.mult)
                    turn_read(ins, ("m", b, i))

            dv.wait_ge(bank_full, IN_T * EV)
            for h in range(H):
                link(V.scalar_tensor_tensor(out=head_bias, in0=delta, scalar=-2.0 ** -(h + 1), in1=count_ln,
                                            op0=ALU.mult, op1=ALU.add))
                for qi in range(NB_P):
                    dv.wait_ge(s_full, NB_P * h + qi + 1)
                    if h and qi == 0:
                        for j in range(NB_P):
                            bank, n = turn(("p", h - 1, j))
                            dv.wait_ge(turn_full[bank - 5], n + 1)
                    n = (qi + 1) * P
                    V.scalar_tensor_tensor(out=prob[qi], in0=ps[:, qi, 0:n], scalar=SCALE, in1=head_bias[:, SEQ - n:SEQ],
                                           op0=ALU.mult, op1=ALU.add).then_inc(s_free, 1)
                    dv.wait_ge(s_free, NB_P * h + qi + 1)
                    link(V.reduce_max(stat[:, 32 + qi:33 + qi], prob[qi], AX_X))
                V.tensor_scalar(stat[:, 32:36], stat[:, 32:36], -1.0, None, ALU.mult).then_inc(biased, 1)
                dv.wait_ge(exped, NB_P * (h + 1))
                link(V.reciprocal(stat[:, 36:40], stat[:, 36:40]))
                for qi in range(NB_P):
                    V.tensor_scalar(prob[qi], prob[qi], stat[:, 36 + qi:37 + qi], None, ALU.mult).then_inc(normed, 1)
                dv.wait_ge(normed, NB_P * (h + 1))

            dv.wait_ge(o_full, H)
            dv.wait_ge(kv_stored, 16 * 2 * BLOCKS)
            for par in range(2):
                link(V.memset(q_mask[par], 0.0))
            bank, n = turn(("qs",))
            dv.wait_ge(turn_free[bank - 5], n + 1)

            def mask_queries(b):
                m = q_mask[b % 2]
                own = bass.AP(m.tensor, m.offset, [m.ap[0], [NS + DECT, H], [1, DECT]])
                V.tensor_copy(own, q_st[:, :, DECT * b:DECT * b + DECT]).then_inc(q_masked, 1)

            def turn_key(b, h, i):
                if i == 0 and b * H + h >= 2:
                    dv.wait_ge(ss_full, b * H + h - 1)
                if (h + i) % 2 == 1:
                    n = min(512, NK - 512 * i)
                    bank = wait_turn_full(dv, ("kt", b, h, i))
                    turn_read(V.tensor_copy(key_t[h % 2][:, 512 * i:512 * i + n], ps[:, bank, 0:n]), ("kt", b, h, i))

            mask_queries(0)
            p = prob_s
            for b in range(DECB):
                for h in range(2 if b else 0, H):
                    for i in range(2):
                        turn_key(b, h, i)
                dv.wait_ge(ss_full, H * (b + 1))
                for j, (lo, n) in enumerate(((0, 512), (512, NK - 512))):
                    V.scalar_tensor_tensor(out=p[:, lo:lo + n], in0=ps[:, j, 0:n], scalar=SCALE,
                                           in1=bias_s[:, lo:lo + n], op0=ALU.mult, op1=ALU.add)
                V.scalar_tensor_tensor(out=p[:, NK:NKS], in0=ps[:, 2, 0:NS], scalar=SCALE, in1=bias_new[:, b, :],
                                       op0=ALU.mult, op1=ALU.add).then_inc(ss_free, 1)
                dv.wait_ge(ss_free, b + 1)
                link(V.reduce_max(stat[:, 40:41], p, AX_X))
                V.tensor_scalar(stat[:, 40:41], stat[:, 40:41], -1.0, None, ALU.mult).then_inc(s_biased, 1)
                if b + 1 < DECB:
                    mask_queries(b + 1)
                    for h in range(2):
                        for i in range(2):
                            turn_key(b + 1, h, i)
                dv.wait_ge(s_exped, b + 1)
                link(V.reciprocal(stat[:, 41:42], stat[:, 41:42]))
                V.tensor_scalar(p, p, stat[:, 41:42], None, ALU.mult).then_inc(s_normed, 1)
                bank = wait_turn_full(dv, ("pt", b, 0))
                turn_read(V.tensor_copy(prob_st[:, 0:4, :], ps[:, bank, :].rearrange("p (c n) -> p c n", n=P)), ("pt", b, 0))

            dv.wait_ge(x1_loaded, 16 * BLOCKS)
            dv.wait_ge(mod2_loaded, 16 * 6)
            for n in range(OUT_T):
                dv.wait_ge(bank_full, (IN_T + n) * EV + 1)
                V.tensor_copy(partial, ps[:, 4, :]).then_inc(bank_free, 1)
                for i, b in enumerate((0, NB_P, 1, 2, 3)):
                    r = ROWS[b]
                    e = n * BLOCKS + i
                    cols = slice(n * NC, (n + 1) * NC)
                    gate = gate1_p if b < NB_P else gate1_s
                    pt = gated[e % 2][0:r, :]
                    dv.wait_ge(bank_full, (IN_T + n) * EV + EV_OF[b] + 1)
                    if e >= 2:
                        dv.wait_ge(x1_done, e - 1)
                    V.tensor_tensor(pt, ps[0:r, BANK_OF[b], :], gate[0:r, cols], ALU.mult).then_inc(bank_free, 1)
                    dv.wait_ge(bank_free, EV + (IN_T + n) * EV + EV_OF[b] + 1)
                    V.tensor_tensor(x1[0:r, b, cols], x1[0:r, b, cols], pt, ALU.add).then_inc(x1_done, 1)
            for b in range(BLOCKS):
                norm(BLOCKS + b, x1[:, b, :], h2[b], b, *((scale2_p, shift2_p) if b < NB_P else (scale2_s, shift2_s)))

            dv.wait_ge(norm_h, 2 * BLOCKS)
            for v in (top_s, top_i.bitcast(F32), best_s, best_j.bitcast(F32)):
                link(V.memset(v, 0.0))

            def wave(make):
                done = []
                for b in range(BLOCKS):
                    make(b).then_inc(dve, 1)
                    chain[0] += 1
                    done.append(chain[0])
                return done

            def top16(values, scratch, out_s, out_i):
                rs = [slice(0, ROWS[b]) for b in range(BLOCKS)]

                def after(done, f):
                    def make(b):
                        dv.wait_ge(dve, done[b])
                        return f(b, rs[b])
                    return make

                d = wave(lambda b: V.max(out_s(b)[rs[b], 0:8], values(b)))
                i1 = wave(after(d, lambda b, r: V.max_index(out_i(b)[r, 0:8], out_s(b)[r, 0:8], values(b))))
                d = wave(after(d, lambda b, r: V.match_replace(scratch(b)[r, :], out_s(b)[r, 0:8], values(b), -3.0e38)))
                d = wave(after(d, lambda b, r: V.max(out_s(b)[r, 8:16], scratch(b)[r, :])))
                wave(after(d, lambda b, r: V.max_index(out_i(b)[r, 8:16], out_s(b)[r, 8:16], scratch(b)[r, :])))
                dv.wait_ge(dve, chain[0])

            wide = [P, BLOCKS, TOPK, TOPK]
            as4 = lambda v: v.rearrange("p b (k a) -> p b k a", a=TOPK)
            for h in range(PH):
                cols = slice(h * TOPK, (h + 1) * TOPK)
                for j in range(2):
                    dv.wait_ge(sc_full, h * 2 + j + 1)
                    top16(lambda b: ps[0:P, 4 + 2 * j, b * NKEY:(b + 1) * NKEY] if b < NB_P else ps[0:NS, 5 + 2 * j, 0:NKEY],
                          lambda b: cut[:, b, :], lambda b: top_s[:, b, j, :], lambda b: top_i[:, b, j, :])
                    dv.sem_inc(sc_free, 1)
                link(V.tensor_copy(top_f, top_i))
                link(V.tensor_tensor(as4(cand), top_s[:, :, 0, :].unsqueeze(3).broadcast_to(wide),
                                     top_s[:, :, 1, :].unsqueeze(2).broadcast_to(wide), ALU.add))
                top16(lambda b: cand[0:ROWS[b], b, :], lambda b: cand_cut[:, b, :], lambda b: best_s[:, b, :], lambda b: best_j[:, b, :])
                link(V.tensor_tensor(gate_all[:, :, cols], best_s, best_s[:, :, 0:1].broadcast_to([P, BLOCKS, TOPK]), ALU.subtract))
                link(V.tensor_scalar(best_ab[0], best_j, 4, None, ALU.logical_shift_right))
                link(V.tensor_scalar(best_ab[1], best_j, TOPK - 1, None, ALU.bitwise_and))
                for j in range(2):
                    link(V.tensor_copy(best_abf[j], best_ab[j]))
                    link(V.tensor_tensor(as4(pick[j]), best_abf[j].unsqueeze(3).broadcast_to(wide),
                                         iota16.unsqueeze(1).unsqueeze(1).broadcast_to(wide), ALU.is_equal))
                    link(V.tensor_tensor(as4(pick[j]), as4(pick[j]), top_f[:, :, j, :].unsqueeze(2).broadcast_to(wide), ALU.mult))
                    link(V.reduce_sum(key_f[j], as4(pick[j]), AX_X))
                link(V.scalar_tensor_tensor(out=idx_all[:, :, cols], in0=key_f[0], scalar=float(NKEY), in1=key_f[1],
                                            op0=ALU.mult, op1=ALU.add))
            dv.sem_inc(gates_done, 1)

            dv.wait_ge(gate_exp, 2)
            for r, lo, n in ((P, 0, NB_P), (NS, NB_P, 1)):
                g = gate_all[0:r, lo:lo + n, :].rearrange("p b (h k) -> p (b h) k", k=TOPK)
                s = gate_sum[0:r, 0:n * PH]
                link(V.reduce_sum(s, g, AX_X))
                link(V.reciprocal(s, s))
                link(V.tensor_tensor(g, g, s.unsqueeze(2).broadcast_to([r, n * PH, TOPK]), ALU.mult))
            for half in range(2):
                V.memset(ps[:, 4 * half:4 * half + 4, :].rearrange("p a n -> p (a n)"), 0.0).then_inc(zeroed, 1)
            dv.wait_ge(zeroed, 2)
            dv.sem_inc(gates_done, 1)

            def groups(h_rows, gates, n0, i):
                for par in range(2):
                    n = n0 + par
                    for k in range(GRP):
                        dv.wait_ge(u_loaded[k % RING], (n * 2 + k // RING + 1) * 16)
                        V.tensor_tensor_reduce(out=u_slot[k % RING], in0=u_slot[k % RING], in1=h_rows, scale=1.0, scalar=0.0,
                                               op0=ALU.mult, op1=ALU.add, accum_out=act_sum[:, par, k:k + 1]).then_inc(u_done, 1)
                    dv.wait_ge(gelu_done, n + 1)
                    V.tensor_tensor(coef[:, par, :], act_gelu[:, par, :], gates[:, bass.ds(i * 2 * GRP + par * GRP, GRP)],
                                    ALU.mult).then_inc(coef_done, 1)

            def finish(b):
                r = ROWS[b]
                total = GRP * (1 + (2 * (SLOTS // GRP // 2) * (b + 1) if b < NB_P else 2 * (SLOTS // GRP // 2) * NB_P + 4))
                gate = gate2_p if b < NB_P else gate2_s
                bank = 4 * (b % 2)
                acc = ps[0:r, bank:bank + 4, :].rearrange("p a n -> p (a n)")
                dv.wait_ge(v_done, total)
                link(V.tensor_tensor(acc, acc, gate[0:r, :], ALU.mult))
                V.tensor_tensor(x1[0:r, b, :], x1[0:r, b, :], acc, ALU.add).then_inc(fin_x, 1)
                dv.wait_ge(fin_sq, b + 1)
                if b + 2 < BLOCKS:
                    V.memset(ps[:, bank:bank + 4, :].rearrange("p a n -> p (a n)"), 0.0).then_inc(zeroed, 1)
                s = stat[0:r, 48 + b:49 + b]
                V.tensor_scalar(s, s, 1.0 / D, EPS, ALU.mult, ALU.add).then_inc(fin_ms, 1)
                dv.wait_ge(fin_rt, b + 1)
                link(V.reciprocal(s, s))
                V.scalar_tensor_tensor(out=x1[0:r, b, :], in0=x1[0:r, b, :], scalar=s, in1=g_fin[0:r, :],
                                       op0=ALU.mult, op1=ALU.mult).then_inc(fin_y, 1)

            dv.wait_ge(rep_loaded, 16 * 11)
            dv.wait_ge(peer_tables, 16 * 3)
            pairs = SLOTS // GRP // 2
            for b in range(BLOCKS):
                base = b * 2 * pairs
                gates = gate_all[:, b, :] if b < NB_P else gate_rep
                groups(h2[b], gates, base, 0)
                if b:
                    finish(b - 1)
                with dv.Fori(1, pairs if b < NB_P else pairs // 4) as i:
                    groups(h2[b], gates, i * 2 + base, i)
            finish(NB_P)

        @block.tensor
        def _(pe):
            TT, MM = nc.tensor.transpose, nc.tensor.matmul
            pe.sem_inc(bank_free, EV)
            pe.sem_inc(ada_free, 4)
            pe.sem_inc(v_done, GRP)

            def turn_many(key, pieces):
                bank = wait_turn_free(pe, key)
                at_col = 0
                for src, rows, cols in pieces:
                    ins = TT(ps[0:cols, bank, at_col:at_col + rows], src, ident[0:rows, 0:rows])
                    at_col += rows
                turned(ins, key)

            pe.wait_ge(pool_const, 2)
            pe.wait_ge(silu_done, 1)
            turn_many(("c",), [(c_in[:, k * P:(k + 1) * P], 1 + DECB, P) for k in range(KD)])
            pe.wait_ge(tri_done, 2)
            for i in range(2):
                turn_many(("ws", i), [(ws_in[:, 4 * i + g, :], P, P) for g in range(4)])
            turn_many(("wd",), [(wd_in[:, g, :], NS, NS) for g in range(G)])
            pe.wait_ge(in_misc, 16 * (3 + DECB + 1))
            turn_many(("sk",), [(sub_in[:, j, :], P, P) for j in range(2)])

            bank, n = turn(("c",))
            pe.wait_ge(turn_free[bank - 5], n + 1)
            pe.wait_ge(tables_done, 1)

            def quarters(out, lhs, rhs):
                for k in range(KD):
                    j = k % 4
                    ins = MM(out[QUAD * j:QUAD * j + QUAD], lhs(k), rhs(k), start=(k < 4), stop=(k >= KD - 4))
                return ins

            with pe.Fori(0, ADA_T // 2) as i:
                for s in range(2):
                    pe.wait_ge(w_loaded[s], (i + 1) * 16)
                    pe.wait_ge(ada_free, i * 4 + 2 * s + 1)
                    quarters(ps[:, s, :], lambda k: c_t[:, k, :], lambda k: w_slot[s][:, k, :]).then_inc(ada_full, 1)
                    pe.wait_ge(ada_free, i * 4 + 2 * s + 5)
                    MM(ps[0:QUAD, 2 + s, :], sel, partial, start=True, stop=True).then_inc(ada_full, 1)
            pe.wait_ge(ada_free, 4 + 2 * ADA_T)

            for b in range(BLOCKS):
                pe.wait_ge(norm_h, b + 1)
                for g in range(4):
                    turn_many(("h", b, g), [(h_buf[b][0:ROWS[b], (4 * g + k) * P:(4 * g + k + 1) * P], ROWS[b], P) for k in range(4)])

            def project(lhs, first, uses, pairs, tile0):
                with pe.Fori(0, pairs) as i:
                    for s in range(2):
                        pe.wait_ge(w_loaded[s], (i + uses + 1) * 16)
                        pe.wait_ge(bank_free, (i * 2 + first + s) * EV + 1)
                        quarters(ps[:, 4, :], lambda k: lhs[:, k, tok(NB_P)], lambda k: w_slot[s][:, k, :]).then_inc(bank_full, 1)
                        for b in (0, NB_P, 1, 2, 3):
                            if b == NB_P:
                                pe.wait_ge(bank_free, (i * 2 + first + s + 1) * EV + 1)
                                MM(ps[0:NS, BANK_OF[b], :], sel, partial, start=True, stop=True).then_inc(bank_full, 1)
                                continue
                            pe.wait_ge(bank_free, (i * 2 + first + s) * EV + EV_OF[b] + 1)
                            for k in range(KD):
                                ins = MM(ps[:, BANK_OF[b], :], lhs[:, k, tok(b)], w_slot[s][:, k, :],
                                         start=(k == 0), stop=(k == KD - 1))
                            ins.then_inc(bank_full, 1)

            for key in [("h", NB_P, g) for g in range(4)]:
                bank, n = turn(key)
                pe.wait_ge(turn_free[bank - 5], n + 1)
            project(h_t, 0, A_USES, 2, T_IN)
            pe.wait_ge(bank_free, EV + 4 * EV)
            for b in range(BLOCKS):
                pe.wait_ge(ln_done, b + 1)
                r = ROWS[b]
                for i in range(2):
                    key = ("m", b, i)
                    bank = wait_turn_free(pe, key)
                    for g in range(4):
                        w = ws_t if b < NB_P else wd_t
                        ins = MM(ps[0:r, bank, g * P:(g + 1) * P], w[0:r, 4 * i + g, 0:r],
                                 g_all[0:r, b, (4 * i + g) * P:(4 * i + g + 1) * P], start=True, stop=True)
                    turned(ins, key)
            for b in range(BLOCKS):
                wait_turn_read(pe, ("m", b, 1))
                for i in range(2):
                    turn_many(("mt", b, i), [(u_all[0:ROWS[b], b, (4 * i + g) * P:(4 * i + g + 1) * P], ROWS[b], P) for g in range(4)])
            project(h_t, 4, A_USES + 2, 3, T_IN + 4)

            pe.wait_ge(bank_free, EV + IN_T * EV)

            def scores(h):
                cols = slice(h * DH, (h + 1) * DH)
                turn_many(("q", h), [(q_all[:, b, cols], P, P) for b in range(NB_P)])
                turn_many(("k", h), [(k_all[:, b, cols], P, P) for b in range(NB_P)])
                for key in (("q", h), ("k", h)):
                    bank, n = turn(key)
                    pe.wait_ge(turn_free[bank - 5], n + 1)
                for qi in range(NB_P):
                    if h:
                        pe.wait_ge(s_free, NB_P * (h - 1) + qi + 1)
                    MM(ps[:, qi, 0:(qi + 1) * P], q_t[h % 2][:, qi * P:(qi + 1) * P], k_t[h % 2][:, 0:(qi + 1) * P],
                       start=True, stop=True).then_inc(s_full, 1)

            scores(0)
            for h in range(H):
                if h + 1 < H:
                    scores(h + 1)
                pe.wait_ge(normed, NB_P * (h + 1))
                for j in range(NB_P):
                    turn_many(("p", h, j), [(prob[qi][:, j * P:(j + 1) * P], P, P) for qi in range(j, NB_P)])
                if h:
                    pe.wait_ge(o_free, h)
                for j in range(NB_P):
                    bank, n = turn(("p", h, j))
                    pe.wait_ge(turn_free[bank - 5], n + 1)
                    ins = MM(ps[:, 4, j * P:SEQ], v_all[:, j, h * DH:(h + 1) * DH], prob_t[:, j, j * P:SEQ],
                             start=(j == 0), stop=(j == NB_P - 1))
                ins.then_inc(o_full, 1)

            pe.wait_ge(s_free, NB_P * H)
            turn_many(("qs",), [(q_all[0:NS, NB_P, h * DH:(h + 1) * DH], NS, P) for h in range(H)])
            turn_many(("ks",), [(k_all[0:NS, NB_P, h * DH:(h + 1) * DH], NS, P) for h in range(H)])
            bank, n = turn(("ks",))
            pe.wait_ge(turn_free[bank - 5], n + 1)

            def turn_keys(b, h):
                if h == 0:
                    pe.wait_ge(kvk_loaded[b % 2], 64 * (b // 2 + 1))
                cols = slice(h * DH, (h + 1) * DH)
                turn_many(("kt", b, h, 0), [(kv_k[b % 2][:, c, cols], P, P) for c in range(4)])
                turn_many(("kt", b, h, 1), [(kv_k[b % 2][:, c, cols], P, P) for c in range(4, CH)])

            for h in range(2):
                turn_keys(0, h)
            for b in range(DECB):
                vals = kv_v[b % 2]
                pe.wait_ge(q_masked, b + 1)
                for h in range(H):
                    for i in range(2):
                        wait_turn_read(pe, ("kt", b, h, i))
                    if b and h == 0:
                        pe.wait_ge(ss_free, b)
                    q = q_mask[b % 2][:, h, :]
                    r = slice(QUAD * (h % 4), QUAD * (h % 4) + QUAD)
                    MM(ps[r, 0, :], q, key_t[h % 2][:, 0:512], start=(h < 4), stop=(h >= 4))
                    MM(ps[r, 1, 0:NK - 512], q, key_t[h % 2][:, 512:NK], start=(h < 4), stop=(h >= 4))
                    MM(ps[r, 2, 0:NS], q, k_st[:, h, :], start=(h < 4), stop=(h >= 4)).then_inc(ss_full, 1)
                    if h + 2 < H:
                        turn_keys(b, h + 2)
                if b + 1 < DECB:
                    for h in range(2):
                        turn_keys(b + 1, h)
                pe.wait_ge(s_normed, b + 1)
                turn_many(("pt", b, 0), [(prob_s[:, c * P:(c + 1) * P], P, P) for c in range(4)])
                turn_many(("pt", b, 1), [(prob_s[:, c * P:min((c + 1) * P, NKS)], P, min(P, NKS - c * P)) for c in range(4, CH + 1)])
                for i in range(2):
                    wait_turn_read(pe, ("pt", b, i))
                pe.wait_ge(new_turned, b + 1)
                pe.wait_ge(kvv_loaded[b % 2], 64 * (b // 2 + 1))
                if b:
                    pe.wait_ge(os_free, b)
                for g in range(2):
                    for c in range(CH + 1):
                        rows = slice(0, P if c < CH else NS)
                        for j in range(4):
                            cols = slice((4 * g + j) * DH, (4 * g + j + 1) * DH)
                            ins = MM(ps[QUAD * j:QUAD * j + QUAD, 3, g * P:(g + 1) * P], prob_st[rows, c, QUAD * j:QUAD * j + QUAD],
                                     vals[:, c, cols] if c < CH else v_all[rows, NB_P, cols], start=(c == 0), stop=(c == CH))
                ins.then_inc(os_full, 1)
                pe.wait_ge(os_free, b + 1)
                turn_many(("ot", b), [(att_s[:, g, :], P, P) for g in range(2)])

            wait_turn_read(pe, ("ot", DECB - 1))
            pe.wait_ge(o_free, H)
            project(mix_t, IN_T, A_USES + IN_USES, OUT_T // 2, T_OUT)
            pe.wait_ge(bank_free, EV + (IN_T + OUT_T) * EV)
            for b in range(BLOCKS):
                pe.wait_ge(norm_h, BLOCKS + b + 1)
                for g in range(4):
                    turn_many(("h2", b, g), [(h2[b][0:ROWS[b], (4 * g + k) * P:(4 * g + k + 1) * P], ROWS[b], P) for k in range(4)])
            for g in range(4):
                bank, n = turn(("h2", NB_P, g))
                pe.wait_ge(turn_free[bank - 5], n + 1)

            pe.sem_inc(qry_free, 5)
            pe.sem_inc(sc_free, 2)
            with pe.Fori(0, PH // 2) as i:
                for s in range(2):
                    h = i * 2 + s
                    w = wq_slot[s]
                    pe.wait_ge(w_loaded[s], (i + A_USES + IN_USES + OUT_T // 2 + 1) * 16)
                    pe.wait_ge(qry_free, h * 5 + 1)
                    quarters(ps[:, 1, 0:2 * P], lambda k: h2_t[:, k, SEQ:NTOK], lambda k: w[:, k, :]).then_inc(qry_full, 1)
                    for j in range(2):
                        pe.wait_ge(qry_free, h * 5 + (2 if j == 0 else 5))
                        for k in range(KD):
                            ins = MM(ps[:, 2 * j, :], w[:, k, j * P:(j + 1) * P], h2_t[:, k, 0:SEQ], start=(k == 0), stop=(k == KD - 1))
                        ins.then_inc(qry_full, 1)
                        if j == 0:
                            pe.wait_ge(qry_free, h * 5 + 6)
                            for jj in range(2):
                                ins = MM(ps[:, 3, jj * NS:(jj + 1) * NS], partial[:, jj * P:(jj + 1) * P], sel, start=True, stop=True)
                            ins.then_inc(qry_full, 1)
                    for j in range(2):
                        pe.wait_ge(qry_free, h * 5 + (8 if j == 0 else 10))
                        pe.wait_ge(sc_free, h * 2 + j + 1)
                        for b in range(BLOCKS):
                            out = ps[0:ROWS[b], 4 + 2 * j, b * NKEY:(b + 1) * NKEY] if b < NB_P else ps[0:NS, 5 + 2 * j, 0:NKEY]
                            ins = MM(out, qry_t[j][:, tok(b)], sub_t[:, j, :], start=True, stop=True)
                        ins.then_inc(sc_full, 1)

            def groups(n0, bank, rows):
                for par in range(2):
                    n = n0 + par
                    for k in range(GRP):
                        pe.wait_ge(diag_done, n * GRP + k + 1)
                        pe.wait_ge(v_loaded[k % RING], (n * 2 + k // RING + 1) * 16)
                        for c in range(4):
                            ins = MM(ps[0:rows, bank + c, :], diag[k][:, 0:rows], v_slot[k % RING][:, c * NC:(c + 1) * NC],
                                     start=False, stop=False, skip_group_check=True)
                        ins.then_inc(v_done, 1)

            pairs = SLOTS // GRP // 2
            for b in range(BLOCKS):
                pe.wait_ge(zeroed, 2 if b < 2 else b + 1)
                with pe.Fori(0, pairs if b < NB_P else pairs // 4) as i:
                    groups(i * 2 + b * 2 * pairs, 4 * (b % 2), ROWS[b])


_INS = ["x_prompt", "x_sample", "cache_k", "cache_v", "c_prompt", "c_sample", "w_ada", "b_ada", "g_norm1", "w_in",
        "ln_v_g", "ln_v_b", "w_spatial", "b_spatial", "w_out", "g_norm2", "w_query", "sub_keys", "expert_u",
        "expert_v", "g_final"]
_OUTS = [(1, SEQ, D), (DECB, DECT, D), (1, 1, SEQ, H, DH), (1, 1, SEQ, H, DH), (1, DECB, DECT, H, DH),
         (1, DECB, DECT, H, DH), (1, DECB, DECT, AW)]


def kernel(**inputs):
    import numpy as _np
    import concourse.bacc as _bacc
    from concourse.bass_utils import run_bass_kernel_spmd as _run

    nc = _bacc.Bacc("TRN2", target_bir_lowering=False, num_devices=1)
    arrays, args = {}, []
    for name in _INS:
        a = _np.ascontiguousarray(inputs[name])
        arrays[f"in_{name}_dram"] = a
        args.append(nc.dram_tensor(f"in_{name}_dram", a.shape, mybir.dt.from_np(a.dtype), kind="ExternalInput").ap())
    for i, shape in enumerate(_OUTS):
        args.append(nc.dram_tensor(f"out_{i}_dram", shape, F32, kind="ExternalOutput").ap())
    trunk_step(nc, *args)
    r = _run(nc, [arrays], core_ids=[0])
    return tuple(r.results[0][f"out_{i}_dram"] for i in range(len(_OUTS)))
```
